# Optimizing a Trainium2 kernel written in Bass

```python
import jax, jax.numpy as jnp
from jax import lax
import numpy as np
import math

D_MODEL = 1024
BATCH = 1
SEQ = 256
DEPTH = 2

N_MIXERS = 2
N_META = 16
N_HEADS = 16
QK_NOPE_DIM = 64
QK_ROPE_DIM = 32
QK_HEAD_DIM = QK_NOPE_DIM + QK_ROPE_DIM
V_HEAD_DIM = 64
Q_LORA_RANK = 384
KV_LORA_RANK = 256
ROPE_THETA = 10000.0
Q_BLOCK = 128
POOL_WINDOWS = (2, 4, 8, 16)
N_POOL_GROUPS = len(POOL_WINDOWS)
POOL_GROUP_DIM = D_MODEL // N_POOL_GROUPS
D_FF = 2816
CONV_WIDTH = 3
NORM_EPS = 1e-6
N_MLA_LAYERS = len(range(0, DEPTH, N_MIXERS))
N_POOL_LAYERS = DEPTH - N_MLA_LAYERS


def rmsnorm(x, g):
    xf = x.astype(jnp.float32)
    y = xf * lax.rsqrt(jnp.mean(xf * xf, axis=-1, keepdims=True) + NORM_EPS)
    return (y * g.astype(jnp.float32)).astype(x.dtype)

def rope_tables(length):
    inv = 1.0 / (ROPE_THETA ** (jnp.arange(0, QK_ROPE_DIM, 2, dtype=jnp.float32) / QK_ROPE_DIM))
    ang = jnp.arange(length, dtype=jnp.float32)[:, None] * inv[None, :]
    return jnp.cos(ang), jnp.sin(ang)

def apply_rope(x, cos, sin):
    xf = x.astype(jnp.float32)
    x1, x2 = jnp.split(xf, 2, axis=-1)
    c = cos[None, :, None, :]
    s = sin[None, :, None, :]
    return jnp.concatenate([x1 * c - x2 * s, x2 * c + x1 * s], axis=-1).astype(x.dtype)

def mla_mixer(h, w_dqkv, q_norm, w_uq, kv_norm, w_ukv, w_o, cos, sin):
    B, L, _ = h.shape
    a = h @ w_dqkv
    c_q, c_kv, k_rope = jnp.split(a, [Q_LORA_RANK, Q_LORA_RANK + KV_LORA_RANK], axis=-1)
    c_q = rmsnorm(c_q, q_norm)
    c_kv = rmsnorm(c_kv, kv_norm)
    q = (c_q @ w_uq).reshape(B, L, N_HEADS, QK_HEAD_DIM)
    q = jnp.concatenate([q[..., :QK_NOPE_DIM], apply_rope(q[..., QK_NOPE_DIM:], cos, sin)], axis=-1)
    kv = (c_kv @ w_ukv).reshape(B, L, N_HEADS, QK_NOPE_DIM + V_HEAD_DIM)
    k_nope, v = jnp.split(kv, [QK_NOPE_DIM], axis=-1)
    k_rope = apply_rope(k_rope[:, :, None, :], cos, sin)
    k = jnp.concatenate([k_nope, jnp.broadcast_to(k_rope, (B, L, N_HEADS, QK_ROPE_DIM))], axis=-1)
    scale = QK_HEAD_DIM ** -0.5
    outs = []
    for start in range(0, L, Q_BLOCK):
        end = start + Q_BLOCK
        qb = q[:, start:end]
        kb = k[:, :end]
        vb = v[:, :end]
        s = jnp.einsum('bqhd,bkhd->bhqk', qb, kb).astype(jnp.float32) * scale
        mask = jnp.arange(start, end)[:, None] >= jnp.arange(end)[None, :]
        s = jnp.where(mask[None, None], s, -jnp.inf)
        p = jax.nn.softmax(s, axis=-1).astype(vb.dtype)
        outs.append(jnp.einsum('bhqk,bkhd->bqhd', p, vb))
    o = jnp.concatenate(outs, axis=1).reshape(B, L, N_HEADS * V_HEAD_DIM)
    return o @ w_o

def pool_mixer(h, w_group, scale):
    B, L, D = h.shape
    hf = h.astype(jnp.float32).reshape(B, L, N_POOL_GROUPS, POOL_GROUP_DIM)
    csum = jnp.cumsum(hf, axis=1)
    t = jnp.arange(1, L + 1, dtype=jnp.float32)
    means = []
    for g, w in enumerate(POOL_WINDOWS):
        cg = csum[:, :, g, :]
        prev = jnp.pad(cg[:, :L - w], ((0, 0), (w, 0), (0, 0)))
        cnt = jnp.minimum(t, float(w))[None, :, None]
        means.append((cg - prev) / cnt)
    pooled = jnp.stack(means, axis=2)
    mixed = (pooled - hf).astype(h.dtype)
    y = jnp.einsum('blgc,gcd->blgd', mixed, w_group).reshape(B, L, D)
    return y * scale

def conv_ffn(h, w_up, conv_w, conv_b, w_down):
    L = h.shape[1]
    u = h @ w_up
    up = jnp.pad(u, ((0, 0), (CONV_WIDTH - 1, 0), (0, 0)))
    u = conv_b + sum(conv_w[j] * up[:, j:j + L] for j in range(CONV_WIDTH))
    gate, val = jnp.split(u, 2, axis=-1)
    return (jax.nn.silu(gate) * val) @ w_down

def first_inputs(seed: int = 0) -> dict:
    key = jax.random.key(seed)
    ks = jax.random.split(key, 24)
    f32 = jnp.float32

    def nrm(k, shape, fan_in):
        return jax.random.normal(k, shape, f32) * (fan_in ** -0.5)

    def gain(k, shape, s=0.05):
        return 1.0 + s * jax.random.normal(k, shape, f32)

    return {
        "x": jax.random.normal(ks[0], (BATCH, SEQ, D_MODEL), f32),
        "meta_tokens": jax.random.normal(ks[1], (N_META, D_MODEL), f32),
        "norm_mix_pre": gain(ks[2], (DEPTH, D_MODEL)),
        "norm_mix_post": gain(ks[3], (DEPTH, D_MODEL)),
        "norm_ffn_pre": gain(ks[4], (DEPTH, D_MODEL)),
        "norm_ffn_post": gain(ks[5], (DEPTH, D_MODEL)),
        "mla_w_dqkv": nrm(ks[6], (N_MLA_LAYERS, D_MODEL, Q_LORA_RANK + KV_LORA_RANK + QK_ROPE_DIM), D_MODEL),
        "mla_q_norm": gain(ks[7], (N_MLA_LAYERS, Q_LORA_RANK)),
        "mla_w_uq": nrm(ks[8], (N_MLA_LAYERS, Q_LORA_RANK, N_HEADS * QK_HEAD_DIM), Q_LORA_RANK),
        "mla_kv_norm": gain(ks[9], (N_MLA_LAYERS, KV_LORA_RANK)),
        "mla_w_ukv": nrm(ks[10], (N_MLA_LAYERS, KV_LORA_RANK, N_HEADS * (QK_NOPE_DIM + V_HEAD_DIM)), KV_LORA_RANK),
        "mla_w_o": nrm(ks[11], (N_MLA_LAYERS, N_HEADS * V_HEAD_DIM, D_MODEL), N_HEADS * V_HEAD_DIM),
        "pool_w_group": nrm(ks[12], (N_POOL_LAYERS, N_POOL_GROUPS, POOL_GROUP_DIM, POOL_GROUP_DIM), POOL_GROUP_DIM),
        "pool_scale": gain(ks[13], (N_POOL_LAYERS, D_MODEL), 0.1),
        "ffn_w_up": nrm(ks[14], (DEPTH, D_MODEL, 2 * D_FF), D_MODEL),
        "ffn_conv_w": nrm(ks[15], (DEPTH, CONV_WIDTH, 2 * D_FF), CONV_WIDTH),
        "ffn_conv_b": 0.01 * jax.random.normal(ks[16], (DEPTH, 2 * D_FF), f32),
        "ffn_w_down": nrm(ks[17], (DEPTH, D_FF, D_MODEL), D_FF),
    }

def first_block(x, meta_tokens, norm_mix_pre, norm_mix_post, norm_ffn_pre, norm_ffn_post,
              mla_w_dqkv, mla_q_norm, mla_w_uq, mla_kv_norm, mla_w_ukv, mla_w_o,
              pool_w_group, pool_scale, ffn_w_up, ffn_conv_w, ffn_conv_b, ffn_w_down):
    B, S, D = x.shape
    L = N_META + S
    L_pad = -(-L // Q_BLOCK) * Q_BLOCK
    meta = jnp.broadcast_to(meta_tokens.astype(x.dtype)[None], (B, N_META, D))
    h = jnp.concatenate([meta, x, jnp.zeros((B, L_pad - L, D), x.dtype)], axis=1)
    cos, sin = rope_tables(L_pad)
    for i in range(DEPTH):
        j = i // N_MIXERS
        a = rmsnorm(h, norm_mix_pre[i])
        if i % N_MIXERS == 0:
            m = mla_mixer(a, mla_w_dqkv[j], mla_q_norm[j], mla_w_uq[j], mla_kv_norm[j],
                          mla_w_ukv[j], mla_w_o[j], cos, sin)
        else:
            m = pool_mixer(a, pool_w_group[j], pool_scale[j])
        h = h + rmsnorm(m, norm_mix_post[i])
        f = conv_ffn(rmsnorm(h, norm_ffn_pre[i]), ffn_w_up[i], ffn_conv_w[i], ffn_conv_b[i], ffn_w_down[i])
        h = h + rmsnorm(f, norm_ffn_post[i])
    return h[:, N_META:L]


DEPTH_2 = 1

GLA_HEADS = 4
GLA_DK = 64
GLA_DV = 128
GLA_QK_DIM = GLA_HEADS * GLA_DK
GLA_V_DIM = GLA_HEADS * GLA_DV
GATE_RANK = 16
GATE_NORMALIZER = 16.0
CHUNK = 64
CONV_DIM = 512
IN_SPLITS = (GLA_QK_DIM, GLA_QK_DIM, GLA_V_DIM, GLA_V_DIM, GATE_RANK, CONV_DIM, CONV_DIM, CONV_DIM)
IN_DIM = sum(IN_SPLITS)
MIX_DIM = GLA_V_DIM + CONV_DIM
FFN_HIDDEN = int(math.ceil(8 * D_MODEL / 3 / 256) * 256)
PLE_DIM = 256


def _rmsnorm(x, g):
    xf = x.astype(jnp.float32)
    xf = xf * lax.rsqrt(jnp.mean(xf * xf, axis=-1, keepdims=True) + NORM_EPS)
    return (xf * g.astype(jnp.float32)).astype(x.dtype)

def _gla_chunked(q, k, v, log_a):
    b_, s_, h_, dk = q.shape
    dv = v.shape[-1]
    n = s_ // CHUNK

    def to_chunks(t):
        return t.reshape(b_, n, CHUNK, h_, t.shape[-1]).transpose(1, 0, 3, 2, 4)

    causal = jnp.tril(jnp.ones((CHUNK, CHUNK), dtype=bool))[:, :, None]

    def step(state, inp):
        qc, kc, vc, gc = inp
        bcum = jnp.cumsum(gc, axis=2)
        diff = bcum[:, :, :, None, :] - bcum[:, :, None, :, :]
        decay = jnp.where(causal, jnp.exp(jnp.where(causal, diff, 0.0)), 0.0)
        scores = jnp.einsum('bhtd,bhsd,bhtsd->bhts', qc, kc, decay)
        o_intra = jnp.einsum('bhts,bhsv->bhtv', scores, vc)
        o_inter = jnp.einsum('bhtd,bhdv->bhtv', qc * jnp.exp(bcum), state)
        b_last = bcum[:, :, -1, :]
        k_dec = kc * jnp.exp(b_last[:, :, None, :] - bcum)
        new_state = jnp.exp(b_last)[..., None] * state + jnp.einsum('bhsd,bhsv->bhdv', k_dec, vc)
        return new_state, o_intra + o_inter

    s0 = jnp.zeros((b_, h_, dk, dv), jnp.float32)
    _, o = lax.scan(step, s0, (to_chunks(q), to_chunks(k), to_chunks(v), to_chunks(log_a)))
    return o.transpose(1, 0, 3, 2, 4).reshape(b_, s_, h_, dv)

def _causal_depthwise_conv(u, w):
    return lax.conv_general_dilated(
        u, w[:, None, :].astype(u.dtype), window_strides=(1,),
        padding=[(CONV_WIDTH - 1, 0)],
        dimension_numbers=('NWC', 'WIO', 'NWC'),
        feature_group_count=u.shape[-1])

def second_inputs(seed: int = 0) -> dict:
    key = jax.random.key(seed)
    ks = jax.random.split(key, 20)
    nrm = lambda k, shape, scale: jax.random.normal(k, shape, jnp.float32) * scale
    gain = lambda k, shape: 1.0 + 0.05 * jax.random.normal(k, shape, jnp.float32)
    return {
        "x": nrm(ks[0], (BATCH, SEQ, D_MODEL), 1.0),
        "p": nrm(ks[1], (DEPTH_2, BATCH, SEQ, PLE_DIM), 1.0),
        "ln1_g": gain(ks[2], (DEPTH_2, D_MODEL)),
        "w_in": nrm(ks[3], (DEPTH_2, D_MODEL, IN_DIM), D_MODEL ** -0.5),
        "w_gate_up": nrm(ks[4], (DEPTH_2, GATE_RANK, GLA_QK_DIM), GATE_RANK ** -0.5),
        "b_gate": nrm(ks[5], (DEPTH_2, GLA_QK_DIM), 0.1),
        "conv_w": nrm(ks[6], (DEPTH_2, CONV_WIDTH, CONV_DIM), CONV_WIDTH ** -0.5),
        "gn_g": gain(ks[7], (DEPTH_2, GLA_DV)),
        "w_out": nrm(ks[8], (DEPTH_2, MIX_DIM, D_MODEL), MIX_DIM ** -0.5),
        "ln2_g": gain(ks[9], (DEPTH_2, D_MODEL)),
        "w_gate_upffn": nrm(ks[10], (DEPTH_2, D_MODEL, 2 * FFN_HIDDEN), D_MODEL ** -0.5),
        "w_down": nrm(ks[11], (DEPTH_2, FFN_HIDDEN, D_MODEL), FFN_HIDDEN ** -0.5),
        "ln3_g": gain(ks[12], (DEPTH_2, D_MODEL)),
        "w_ple_gate": nrm(ks[13], (DEPTH_2, D_MODEL, D_MODEL), D_MODEL ** -0.5),
        "w_ple_proj": nrm(ks[14], (DEPTH_2, PLE_DIM, D_MODEL), PLE_DIM ** -0.5),
        "lnf_g": gain(ks[15], (D_MODEL,)),
    }

def second_block(x, p, ln1_g, w_in, w_gate_up, b_gate, conv_w, gn_g, w_out, ln2_g,
              w_gate_upffn, w_down, ln3_g, w_ple_gate, w_ple_proj, lnf_g):
    b_, s_, _ = x.shape
    offsets = list(np.cumsum(IN_SPLITS)[:-1])
    h = x
    for i in range(DEPTH_2):
        u = _rmsnorm(h, ln1_g[i])
        proj = u @ w_in[i]
        q, k, v, g, g_lr, cb, cc, cx = jnp.split(proj, offsets, axis=-1)

        gate_logits = (g_lr @ w_gate_up[i] + b_gate[i]).astype(jnp.float32)
        log_a = jax.nn.log_sigmoid(gate_logits) / GATE_NORMALIZER
        qh = q.astype(jnp.float32).reshape(b_, s_, GLA_HEADS, GLA_DK) * (GLA_DK ** -0.5)
        kh = k.astype(jnp.float32).reshape(b_, s_, GLA_HEADS, GLA_DK)
        vh = v.astype(jnp.float32).reshape(b_, s_, GLA_HEADS, GLA_DV)
        ah = log_a.reshape(b_, s_, GLA_HEADS, GLA_DK)
        o = _gla_chunked(qh, kh, vh, ah).astype(x.dtype)
        gh = g.reshape(b_, s_, GLA_HEADS, GLA_DV)
        o = _rmsnorm(o, gn_g[i]) * jax.nn.silu(gh)
        o = o.reshape(b_, s_, GLA_V_DIM)

        y = cb * _causal_depthwise_conv(cc * cx, conv_w[i])

        mix = jnp.concatenate([o, y], axis=-1) @ w_out[i]
        h = h + mix

        u2 = _rmsnorm(h, ln2_g[i])
        a, bb = jnp.split(u2 @ w_gate_upffn[i], 2, axis=-1)
        h = h + (jax.nn.silu(a) * bb) @ w_down[i]

        u3 = _rmsnorm(h, ln3_g[i])
        gate = jax.nn.sigmoid(u3 @ w_ple_gate[i])
        h = h + gate * (p[i] @ w_ple_proj[i])
    return _rmsnorm(h, lnf_g)


def setup_inputs(seed=0):
    out = dict(first_inputs(seed))
    for name, value in second_inputs(seed + 1).items():
        if name != "x":
            out[name + "_2"] = value
    return out


def reference(
    x, meta_tokens, norm_mix_pre, norm_mix_post, norm_ffn_pre, norm_ffn_post, mla_w_dqkv,
    mla_q_norm, mla_w_uq, mla_kv_norm, mla_w_ukv, mla_w_o, pool_w_group, pool_scale, ffn_w_up,
    ffn_conv_w, ffn_conv_b, ffn_w_down, p_2, ln1_g_2, w_in_2, w_gate_up_2, b_gate_2, conv_w_2,
    gn_g_2, w_out_2, ln2_g_2, w_gate_upffn_2, w_down_2, ln3_g_2, w_ple_gate_2, w_ple_proj_2,
    lnf_g_2,
):
    x = first_block(
        x, meta_tokens, norm_mix_pre, norm_mix_post, norm_ffn_pre, norm_ffn_post, mla_w_dqkv,
        mla_q_norm, mla_w_uq, mla_kv_norm, mla_w_ukv, mla_w_o, pool_w_group, pool_scale,
        ffn_w_up, ffn_conv_w, ffn_conv_b, ffn_w_down,
    )
    return second_block(
        x, p_2, ln1_g_2, w_in_2, w_gate_up_2, b_gate_2, conv_w_2, gn_g_2, w_out_2, ln2_g_2,
        w_gate_upffn_2, w_down_2, ln3_g_2, w_ple_gate_2, w_ple_proj_2, lnf_g_2,
    )


_drawn_inputs = setup_inputs


def setup_inputs(seed=0):
    import zlib

    import numpy as np

    out = dict(_drawn_inputs(seed))
    spreads = {}
    factors = {'ffn_conv_b': 4.541, 'b_gate_2': 7.221, 'gn_g_2': 7.096, 'ln2_g_2': 3.187, 'ln3_g_2': 8.0}
    for name, (base, spread) in spreads.items():
        noise = np.random.default_rng([zlib.crc32(name.encode()), seed]).standard_normal(out[name].shape)
        drawn = base * np.exp(spread * noise) if base else spread * noise
        out[name] = __import__('jax').numpy.asarray(drawn.astype(out[name].dtype))
    for name, factor in factors.items():
        out[name] = (out[name] * factor).astype(out[name].dtype)
    return out
```

```python
from contextlib import ExitStack

import numpy as np

import concourse.bass as bass
from concourse import mybir

F32 = mybir.dt.float32
F32R = mybir.dt.float32r
I32 = mybir.dt.int32
ALU = mybir.AluOpType
ACT = mybir.ActivationFunctionType
AX = mybir.AxisListType.X

LOOPED = ("e", "fpost0", "fpost1")
P = 128
D = 1024
DC = D // P
META, SEQ = 16, 256
T1 = META + SEQ
FF = 2816
FC = FF // P
NH, NOPE, ROPE, VD = 16, 64, 32, 64
QR, KVR = 384, 256
QC, KC = QR // P, KVR // P
TQ = 96
QT = [(0, 96), (96, 96), (192, 80)]
PTOFF = [0, T1, T1 + 176]
SCALE = float(NOPE + ROPE) ** -0.5
EPS = 1e-6
WINDOWS = (2, 4, 8, 16)
GH, GDK, GDV = 4, 64, 128
FAR, DIAGONAL = 7, 8
LEVEL_ORDER = [DIAGONAL] + list(range(8))
FIRST_LEVEL = LEVEL_ORDER[0]
LEVEL_BEFORE = {b: a for a, b in zip(LEVEL_ORDER, LEVEL_ORDER[1:])}
SLOT = 24 * P
NORM_BANK, R_BANK = 6, 7

PCOLS = {}


def _place(names):
    at = 0
    for name, n in names:
        PCOLS[name] = at
        at += n
    return at


NPAR = _place([("mix_pre0", 8), ("mix_pre1", 8), ("mix_post0", 8), ("mix_post1", 8),
               ("ffn_pre0", 8), ("ffn_pre1", 8), ("ffn_post0", 8), ("ffn_post1", 8),
               ("q_norm", QC), ("kv_norm", KC), ("pool_scale", 8),
               ("cw0", 3 * 2 * FC), ("cw1", 3 * 2 * FC), ("cb0", 2 * FC), ("cb1", 2 * FC),
               ("ln1", 8), ("ln2", 8), ("ln3", 8), ("lnf", 8),
               ("b_gate", 2), ("conv2", 12), ("gn", 1)])

STREAM = [
    ("dq", 1, 24, 3, "v"), ("dkv", 1, 16, 2, "v"), ("dkr", 1, 16, 2, "v"),
    ("uqn", 1, 24, 8, "a"), ("uqr", 1, 24, 8, "v"), ("uk", 1, 16, 8, "a"), ("uv", 1, 16, 6, "v"),
    ("wo", 4, 16, 2, "a"),
    ("up0", FC, 16, 2, "v"), ("down0", DC, 22, 1, "a"),
    ("pool", 1, 16, 8, "a"),
    ("up1", FC, 16, 2, "v"), ("down1", DC, 22, 1, "a"),
    ("gin_a", 1, 24, 3, "v"), ("gin_k", 1, 16, 2, "v"), ("gin_v", 2, 16, 2, "a"),
    ("gin_g", 2, 16, 2, "v"), ("gin_c", 4, 24, 3, "v"),
    ("wout", 4, 16, 2, "v"),
    ("pproj", 1, 16, 8, "a"),
    ("up2", FC, 16, 2, "v"), ("down2", DC, 22, 1, "v"),
    ("pgate", 4, 16, 2, "v"),
]
FIRST_UNIT, FIRST_BLOCK, UNITS, BLOCKS = {}, {}, [], []
for _name, _units, _tiles, _blocks, _eng in STREAM:
    FIRST_UNIT[_name], FIRST_BLOCK[_name] = len(UNITS), len(BLOCKS)
    for _u in range(_units):
        _n = len(UNITS)
        for _b in range(_blocks):
            BLOCKS.append(dict(unit=_n, eng=_eng, bank=(3 * (_n % 2) + _b) % 6,
                               freed=1 + sum(1 for x in BLOCKS if x["eng"] == _eng)))
        UNITS.append(dict(name=_name, u=_u, tiles=_tiles, first=len(BLOCKS) - _blocks, blocks=_blocks))
BY_NAME = {s[0]: s for s in STREAM}
for _i, _x in enumerate(BLOCKS):
    _x["before"] = next((j for j in range(_i - 1, -1, -1) if BLOCKS[j]["bank"] == _x["bank"]), None)


def vector_cols(n):
    return (3 * UNITS[n]["tiles"] // 4) * P


class Steps:

    def __init__(self, engine, sem, marks):
        self.engine, self.sem, self.marks = engine, sem, marks
        self.n, self.i = 0, None

    def enter(self, label, i):
        self.label, self.i, self.base = label, i, self.n
        self.stride = self.marks.get(("stride", self.engine, label), 1)

    def leave(self, iterations):
        stride = self.n - self.base
        self.marks[("stride", self.engine, self.label)] = stride
        self.n, self.i = self.base + stride * iterations, None

    def step(self, name=None):
        self.n += 1
        if name is not None:
            self.marks[name] = (self.engine, self.n, self.label if self.i is not None else None)
        return self.sem, 1

    def now(self):
        return self.sem, self.n if self.i is None else self.i * self.stride + self.n


def program(nc, dram, marks, final):
    ctx = ExitStack()
    with ctx:
        def sb(name, shape, dt=F32, stack=None):
            return (stack or ctx).enter_context(nc.sbuf_tensor(name, shape, dt))

        def sem(name):
            return ctx.enter_context(nc.semaphore(name))

        step_sems = {e: sem(f"{e}_steps") for e in ("vector", "scalar", "pool", "tensor")}

        def done(name, i=None):
            engine, n, loop = marks.get(name, ("scalar", 1, None))
            stride = marks.get(("stride", engine, loop), 1)
            if final and name not in marks:
                raise KeyError(name)
            if isinstance(i, tuple):
                i, n = i[0], n - i[1] * stride
            return step_sems[engine], n if i is None else i * stride + n

        products = sem("products")
        high_parts, low_parts_v, low_parts_g = sem("high_parts"), sem("low_parts_v"), sem("low_parts_g")
        freed = {"v": sem("freed_v"), "a": sem("freed_a")}
        loaded = [sem("weights_loaded_0"), sem("weights_loaded_1")]
        tables_in = sem("tables_in")
        h_in = [sem(f"h_in_{c}") for c in range(2)]
        p_in = sem("p_in")
        out_written = sem("out_written")

        raw = [sb(f"raw{s}", [P, SLOT]) for s in range(2)]
        wh = [sb(f"w_high{s}", [P, SLOT], F32R) for s in range(2)]
        wl = [sb(f"w_low{s}", [P, SLOT], F32R) for s in range(2)]
        par = sb("par", [P, NPAR])
        ident = sb("ident", [P, P])
        ones = sb("ones", [P, P])
        h = sb("h", [P, DC, T1])
        m = sb("m", [P, DC, T1])
        uh = sb("u_high", [P, DC, T1], F32R)
        ul = sb("u_low", [P, DC, T1], F32R)
        acc = sb("acc", [P, 2, 3 * P])
        sq = sb("sq", [P, 2, T1])
        rows = sb("r_rows", [P, T1])
        nx = sb("norm_x", [P, 8])
        nh = sb("norm_half", [P, 8])
        nt = sb("norm_t", [P, 8])
        ny = sb("norm_y", [P, 8])
        warm = sb("warm", [P, 1])
        psg = sb("pool_gains", [P, 8])
        diag = sb("norm_diag", [P, 8 * P])
        ur = sb("conv_in", [P, 2, 2 + T1])
        cv = sb("conv_out", [P, 2, T1])
        xf = sb("x_full", [P, T1])

        mla = ExitStack()
        Q = sb("q_heads", [96, NH, T1], stack=mla)
        K = sb("k_heads", [96, NH, T1], stack=mla)
        V = sb("v_tokens", [96, 3, D], stack=mla)
        mla.close()
        xh = sb("x_high", [P, FC, T1], F32R)
        xl = sb("x_low", [P, FC, T1], F32R)
        att = ExitStack()
        rope = sb("rope", [P, 2, T1], stack=att)
        ropeR = sb("rope_r", [P, 2, T1], stack=att)
        ra = sb("rope_a", [P, T1], stack=att)
        rb = sb("rope_b", [P, T1], stack=att)
        kr = sb("k_rope", [P, T1], stack=att)
        cmask = sb("causal", [96, 96], stack=att)
        mx = sb("row_max", [96, 2, 3], stack=att)
        nb = sb("neg_max", [96, 2, 3], stack=att)
        sm = sb("row_sum", [96, 2, 3], stack=att)
        rc = sb("row_inv", [96, 2, 3], stack=att)
        Pp = sb("probs", [96, 2, 560], stack=att)
        PT = sb("probs_t", [96, 2, 528], stack=att)
        att.close()
        pl = ExitStack()
        pa = sb("pool_in", [P, 4, 16 + T1], stack=pl)
        pb = sb("pool_sum", [P, 4, 16 + T1], stack=pl)
        icnt = sb("inv_count", [P, 4, T1], stack=pl)
        pl.close()
        gq = sb("gla_q", [P, 512])
        gk = sb("gla_k", [P, 512])
        pre = sb("gla_pre", [P, 512])
        suf = sb("gla_suf", [P, 512])
        eq = sb("gla_exp_pre", [P, 512])
        ek = sb("gla_exp_suf", [P, 512])
        ql = sb("gla_q_level", [P, 512])
        kl = sb("gla_k_level", [P, 512])
        gv = sb("gla_v", [P, 2, 512])
        Sd = sb("gla_s_diag", [P, 2, 4 * P])
        S01 = sb("gla_s_far", [P, 2, 2 * P])
        lmask = sb("level_masks", [P, 8, P], I32)
        wgu = sb("w_gate_up", [16, 256])
        glr = sb("gate_low_rank", [P, 256])

        bank = [ctx.enter_context(nc.psum_tensor(f"bank{b}", [P, 512], F32)) for b in range(8)]

        def pcol(name, j=0, n=1):
            return par[:, bass.ds(PCOLS[name] + j, n)]

        block = ctx.enter_context(nc.Block())

        @block.sync
        def _(sp):
            sp.dma_start(h[:, 0:4, :], dram["h0"][:, 0:4, :]).then_inc(h_in[0], 16)
            sp.dma_start(h[:, 4:8, :], dram["h0"][:, 4:8, :]).then_inc(h_in[1], 16)

            def slot_free(n):
                sp.wait_ge(high_parts, n - 1)
                sp.wait_ge(low_parts_v, n - 1)
                sp.wait_ge(low_parts_g, n - 1)

            for name, units, tiles, _, _ in STREAM:
                n0, cols, src = FIRST_UNIT[name], tiles * P, dram["w_" + name]
                if units < 8:
                    for u in range(units):
                        n = n0 + u
                        if n >= 2:
                            slot_free(n)
                        sp.dma_start(raw[n % 2][:, 0:cols], src[u, :, :]).then_inc(loaded[n % 2], 16)
                        if n == 0:
                            for dst, key in ((par[:, :], "par"), (ident[:, :], "ident"),
                                             (rope[:, :, :], "rope"), (cmask[:, :], "cmask")):
                                sp.dma_start(dst, dram[key]).then_inc(tables_in, 16)
                else:
                    with sp.Fori(0, units // 2) as i:
                        for k in range(2):
                            n = 2 * i + (n0 + k)
                            slot_free(n)
                            sp.dma_start(raw[(n0 + k) % 2][:, 0:cols], src[2 * i + k, :, :])\
                                .then_inc(loaded[(n0 + k) % 2], 16)
                if name == "down0":
                    sp.wait_ge(*done("att out 7 low"))
                    sp.dma_start(icnt[:, :, :], dram["icnt"]).then_inc(tables_in, 16)
                if name == "down1":
                    sp.wait_ge(*done("pool mixed low 3"))
                    sp.wait_ge(*done("pool mixed high 3"))
                    sp.dma_start(lmask[:, :, :], dram["lmask"]).then_inc(tables_in, 16)
                    sp.dma_start(wgu[:, :], dram["wgu"]).then_inc(tables_in, 16)
                if name == "wout":
                    sp.wait_ge(*done("conv y low 3"))
                    sp.dma_start(cv[:, :, 0:SEQ], dram["p_t"]).then_inc(p_in, 16)
            for c in range(2):
                sp.wait_ge(*done(f"final {4 * c + 3}"))
                sp.dma_start(dram["out"][:, 4 * c:4 * c + 4, :], m[:, 4 * c:4 * c + 4, 0:SEQ])\
                    .then_inc(out_written, 16)
            sp.wait_ge(out_written, 32)

        def through(n):
            return UNITS[n]["first"] + UNITS[n]["blocks"]

        def first_half(n):
            return vector_cols(n) // P // 2 * P

        def up_place(j):
            return (j, None) if j < 2 or j >= FC - 2 else (f"k{j % 2}", (j - 2) // 2)

        def up_turns(eng, S, l, turn):
            for j in range(2):
                turn(j, up_place(j), up_place(j - 1) if j else None)
            with eng.Fori(0, (FC - 4) // 2) as i:
                S.enter(f"up{l}", i)
                for k in range(2):
                    turn(2 * i + (2 + k), (f"k{k}", i), ("k0", i) if k else ("k1", (i, 1)))
                S.leave((FC - 4) // 2)
            for j in range(FC - 2, FC):
                turn(j, up_place(j), up_place(j - 1))

        @block.tensor
        def _(pe):
            S = Steps("tensor", step_sems["tensor"], marks)

            def parts_ready(n, i=None):
                at = n + 1 if i is None else 2 * i + (n + 1)
                pe.wait_ge(high_parts, at)
                pe.wait_ge(low_parts_v, at)
                pe.wait_ge(low_parts_g, at)

            def bank_free(b, i=None, stride=0):
                before = BLOCKS[b]["before"]
                if before is not None:
                    x = BLOCKS[before]
                    pe.wait_ge(freed[x["eng"]], x["freed"] if i is None else i * stride + x["freed"])

            def three(out, hi, lo, rhi, rlo, start, stop):
                nc.tensor.matmul(out, hi, rhi, start=start, stop=False)
                nc.tensor.matmul(out, hi, rlo, start=False, stop=False)
                return nc.tensor.matmul(out, lo, rhi, start=False, stop=stop)

            def weights(n, j):
                return wh[n % 2][:, j * P:(j + 1) * P], wl[n % 2][:, j * P:(j + 1) * P]

            def unit(n, T, xs, chunk_ready=None, middle=None, i=None):
                U = UNITS[n]
                nb, kc = U["blocks"], U["tiles"] // U["blocks"]
                parts_ready(n, i)
                for b in range(nb):
                    bank_free(U["first"] + b, i, 2 * nb)
                for k in range(kc):
                    if chunk_ready is not None:
                        chunk_ready(k)
                    if middle is not None and k == kc // 2:
                        middle()
                    for b in range(nb):
                        hi, lo = weights(n, k * nb + b)
                        last = three(bank[BLOCKS[U["first"] + b]["bank"]][:, 0:T], hi, lo,
                                     xs[0][:, k, 0:T], xs[1][:, k, 0:T], k == 0, k == kc - 1)
                        if k == kc - 1:
                            last.then_inc(products, 1)

            def blocks_in_turn(n, T, operands, kc):
                U = UNITS[n]
                parts_ready(n)
                for b in range(U["blocks"]):
                    bank_free(U["first"] + b)
                    for k in range(kc):
                        hi, lo = weights(n, k * U["blocks"] + b)
                        rhi, rlo = operands(b, k)
                        last = three(bank[BLOCKS[U["first"] + b]["bank"]][:, 0:T], hi, lo, rhi, rlo,
                                     k == 0, k == kc - 1)
                    last.then_inc(products, 1)

            def norm_sums(name, after, squares):
                pe.wait_ge(*done(after))
                for c, x in enumerate(squares):
                    last = nc.tensor.matmul(bank[NORM_BANK][:, c:c + 1], x, ones[:, 0:1], start=True, stop=True)
                last.then_inc(*S.step(f"{name} sums"))

            def norm_rows(name, outs):
                pe.wait_ge(*done(f"{name} diagonal"))
                for c, out in enumerate(outs):
                    last = nc.tensor.matmul(out, ones[:, :], diag[:, c * P:c * P + out.shape[1]], start=True, stop=True)
                last.then_inc(*S.step(f"{name} rows"))

            def token_rows(b, n, at=0):
                return [bank[b][:, at + i * P:at + min((i + 1) * P, n)] for i in range(-(-n // P))]

            def u_ready(name):
                def wait(c):
                    i, k = (c // 2, c % 2) if name == "e" and c < DC - 2 else (None, c)
                    pe.wait_ge(*done(f"{name} u high {k}", i))
                    pe.wait_ge(*done(f"{name} u low {k}", i))
                return wait

            def squares(a, n):
                return [acc[:, a, i * P:(i + 1) * P] for i in range(-(-n // P))]

            def ffn_up(l, T, sums_name):
                n0 = FIRST_UNIT[f"up{l}"]
                us = (uh, ul)
                unit(n0, T, us, u_ready(sums_name))
                norm_sums(sums_name, f"{sums_name} squares", squares(0, T))
                unit(n0 + 1, T, us, None, lambda: norm_rows(sums_name, token_rows(R_BANK, T)))
                with pe.Fori(0, (FC - 2) // 2) as i:
                    for k in range(2):
                        unit(n0 + 2 + k, T, us, i=i)

            def ffn_down(l, T):
                n0 = FIRST_UNIT[f"down{l}"]

                def x_ready(j):
                    k, i = up_place(j + 1 if l < 2 else j)
                    pe.wait_ge(*done(f"x high {l} {k}", i))
                    pe.wait_ge(*done(f"x low {l} {k}", i))
                unit(n0, T, (xh, xl), x_ready)
                unit(n0 + 1, T, (xh, xl))
                with pe.Fori(0, (DC - 2) // 2) as i:
                    for k in range(2):
                        unit(n0 + 2 + k, T, (xh, xl), i=i)

            pe.wait_ge(*done("constants"))
            n = FIRST_UNIT["dq"]
            pe.wait_ge(tables_in, 64)
            unit(n, T1, (uh, ul), u_ready("a0"))
            norm_sums("a0", "a0 squares", squares(0, T1))
            unit(n + 1, T1, (uh, ul), None, lambda: norm_rows("a0", token_rows(R_BANK, T1)))
            unit(n + 2, T1, (uh, ul))
            norm_sums("c", "kv squares", squares(0, T1) + squares(1, T1))
            norm_rows("c", token_rows(R_BANK, T1) + token_rows(NORM_BANK, T1, P))
            for k in range(QC):
                u_ready("c")(k)
            for name in ("uqn", "uqr"):
                blocks_in_turn(FIRST_UNIT[name], T1, lambda b, k: (uh[:, k, :], ul[:, k, :]), QC)
            for k in range(QC, QC + KC):
                u_ready("c")(k)
            blocks_in_turn(FIRST_UNIT["uk"], T1, lambda b, k: (uh[:, QC + k, :], ul[:, QC + k, :]), KC)
            n = FIRST_UNIT["uv"]
            parts_ready(n)
            for half in range(2):
                for t, (q0, nq) in enumerate(QT):
                    b = UNITS[n]["first"] + half * 3 + t
                    bank_free(b)
                    out = bank[BLOCKS[b]["bank"]][0:nq, :]
                    for k in range(KC):
                        at = slice(k * D + half * 512, k * D + half * 512 + 512)
                        toks = slice(q0, q0 + nq)
                        nc.tensor.matmul(out, uh[:, QC + k, toks], wh[n % 2][:, at], start=k == 0, stop=False)
                        nc.tensor.matmul(out, uh[:, QC + k, toks], wl[n % 2][:, at], start=False, stop=False)
                        last = nc.tensor.matmul(out, ul[:, QC + k, toks], wh[n % 2][:, at],
                                                start=False, stop=k == KC - 1)
                    last.then_inc(products, 1)

            pe.wait_ge(*done("k rope"))
            pe.wait_ge(freed["v"], BLOCKS[FIRST_BLOCK["uv"] + 5]["freed"])
            for s in range(NH + 2):
                if s < NH:
                    X, Y = bank[s % 2], bank[2 + s % 2]
                    if s >= 2:
                        pe.wait_ge(*done(f"exp {s - 2}"))
                    for out, (q0, nq) in ((X[0:96, 0:96], QT[0]), (X[0:96, 96:288], QT[1]), (Y[0:80, 0:T1], QT[2])):
                        last = nc.tensor.matmul(out, Q[:, s, q0:q0 + nq], K[:, s, 0:q0 + nq], start=True, stop=True)
                    last.then_inc(*S.step(f"scores {s}"))
                if 1 <= s <= NH:
                    g = s - 1
                    pe.wait_ge(*done(f"probs {g}"))
                    if g >= 1:
                        pe.wait_ge(*done(f"transposed a {g - 1}"))
                        pe.wait_ge(*done(f"transposed b {g - 1}"))
                    at = (0, 96, 288)
                    for out, t, c in ((bank[4][0:96, 0:96], 0, 0), (bank[4][0:96, 96:192], 1, 0),
                                      (bank[4][0:96, 192:272], 2, 0), (bank[5][0:96, 0:96], 1, 1),
                                      (bank[5][0:96, 96:176], 2, 1), (bank[5][0:80, 176:256], 2, 2)):
                        nq, nk = QT[t][1], QT[c][1]
                        src = Pp[0:nq, g % 2, at[t] + 96 * c:at[t] + 96 * c + nk]
                        last = nc.tensor.transpose(out, src, ident[0:nq, 0:nq])
                    last.then_inc(*S.step(f"transposes {g}"))
                if s >= 2:
                    g = s - 2
                    pair, half = g // 2, g % 2
                    pe.wait_ge(*done(f"transposed a {g}"))
                    pe.wait_ge(*done(f"transposed b {g}"))
                    if half == 0 and pair >= 2:
                        pe.wait_ge(*done(f"att out {pair - 2} low"))
                    o = bank[6 + pair % 2][64 * half:64 * half + 64, :]
                    for c, (k0, nk) in enumerate(QT):
                        last = nc.tensor.matmul(o[:, k0:T1], V[0:nk, c, g * VD:(g + 1) * VD],
                                                PT[0:nk, g % 2, PTOFF[c]:PTOFF[c] + T1 - k0],
                                                start=c == 0, stop=c == 2)
                    last.then_inc(*S.step(f"values {g}"))

            n = FIRST_UNIT["wo"]

            def att_ready(k):
                pe.wait_ge(*done(f"att out {k} high"))
                pe.wait_ge(*done(f"att out {k} low"))
            for u in range(4):
                unit(n + u, T1, (uh, ul), att_ready if u == 0 else None)
            norm_sums("post0", "post0 squares", squares(0, T1))
            norm_rows("post0", token_rows(R_BANK, T1))
            ffn_up(0, T1, "f0")
            ffn_down(0, T1)
            norm_sums("fpost0", "fpost0 squares", squares(0, T1))
            norm_rows("fpost0", token_rows(R_BANK, T1))

            norm_sums("a1", "a1 squares", squares(0, T1))
            norm_rows("a1", token_rows(R_BANK, T1))
            n = FIRST_UNIT["pool"]
            parts_ready(n)
            for g in range(4):
                pe.wait_ge(*done(f"pool mixed high {g}"))
                pe.wait_ge(*done(f"pool mixed low {g}"))
                for b in range(2 * g, 2 * g + 2):
                    B = UNITS[n]["first"] + b
                    bank_free(B)
                    for k in range(2):
                        hi, lo = weights(n, (g * 2 + k) * 2 + b % 2)
                        last = three(bank[BLOCKS[B]["bank"]][:, 0:T1], hi, lo, uh[:, 2 * g + k, :],
                                     ul[:, 2 * g + k, :], k == 0, k == 1)
                    last.then_inc(products, 1)
            norm_sums("post1", "post1 squares", squares(0, T1))
            norm_rows("post1", token_rows(R_BANK, T1))
            ffn_up(1, T1, "f1")
            ffn_down(1, T1)
            norm_sums("fpost1", "fpost1 squares", squares(0, T1))
            norm_rows("fpost1", token_rows(R_BANK, T1))

            def level(l):
                if l == DIAGONAL:
                    pe.wait_ge(freed["v"], BLOCKS[FIRST_BLOCK["gin_k"] + 1]["freed"])
                    pe.wait_ge(*done("gate inputs"))
                else:
                    pe.wait_ge(*done(f"level {l} q"))
                    pe.wait_ge(*done(f"level {l} k"))
                    pe.wait_ge(*done(f"level {LEVEL_BEFORE[l]} kept 1"))
                qs, ks = (gq, gk) if l == DIAGONAL else (ql, kl)
                for half in range(2):
                    part = slice(64 * half, 64 * half + 64)
                    for pair in range(2):
                        for i in range(2):
                            if l == FAR and i:
                                continue
                            j = 1 if l == FAR else i
                            o = (pair if l == FAR else pair * 2 + i) * P
                            last = nc.tensor.matmul(bank[6 + half][:, o:o + P],
                                                    ks[part, pair * SEQ + i * P:pair * SEQ + (i + 1) * P],
                                                    qs[part, pair * SEQ + j * P:pair * SEQ + (j + 1) * P],
                                                    start=True, stop=True)
                last.then_inc(*S.step(f"level {l} scores"))

            n = FIRST_UNIT["gin_a"]
            T = SEQ
            us = (uh, ul)
            unit(n, T, us, u_ready("g"))
            norm_sums("g", "g squares", squares(0, T))
            unit(n + 1, T, us, None, lambda: norm_rows("g", token_rows(R_BANK, T)))
            pe.wait_ge(freed["v"], BLOCKS[FIRST_BLOCK["gin_a"]]["freed"])
            pe.wait_ge(tables_in, 16 * 7)
            for pair in range(2):
                last = nc.tensor.matmul(bank[6][:, pair * SEQ:(pair + 1) * SEQ], wgu[:, pair * P:(pair + 1) * P],
                                        glr[0:16, :], start=True, stop=True)
            last.then_inc(*S.step("gate logits"))
            for v in range(2):
                n = FIRST_UNIT["gin_v"] + v
                parts_ready(n)
                for t in range(2):
                    b = UNITS[n]["first"] + t
                    bank_free(b)
                    out = bank[BLOCKS[b]["bank"]][:, 0:256]
                    for k in range(DC):
                        toks, at = slice(t * P, (t + 1) * P), slice(k * 256, (k + 1) * 256)
                        nc.tensor.matmul(out, uh[:, k, toks], wh[n % 2][:, at], start=k == 0, stop=False)
                        nc.tensor.matmul(out, uh[:, k, toks], wl[n % 2][:, at], start=False, stop=False)
                        last = nc.tensor.matmul(out, ul[:, k, toks], wh[n % 2][:, at], start=False, stop=k == DC - 1)
                    last.then_inc(products, 1)
            level(LEVEL_ORDER[0])
            for v in range(2):
                unit(FIRST_UNIT["gin_g"] + v, T, us)
                level(LEVEL_ORDER[1 + v])
            for v in range(4):
                unit(FIRST_UNIT["gin_c"] + v, T, us)
                level(LEVEL_ORDER[3 + v])
            level(LEVEL_ORDER[7])
            level(LEVEL_ORDER[8])
            pe.wait_ge(*done(f"level {LEVEL_ORDER[8]} kept 1"))
            pe.wait_ge(freed["a"], BLOCKS[FIRST_BLOCK["gin_v"] + 3]["freed"])
            for head in range(GH):
                pair, half = head // 2, head % 2
                o = bank[6 + pair]
                at, ch = half * SEQ, slice(head * P, (head + 1) * P)
                nc.tensor.matmul(o[:, at:at + P], gv[:, 0, ch], Sd[:, half, pair * 2 * P:(pair * 2 + 1) * P],
                                 start=True, stop=True)
                nc.tensor.matmul(o[:, at + P:at + 2 * P], gv[:, 0, ch], S01[:, half, pair * P:(pair + 1) * P],
                                 start=True, stop=False)
                last = nc.tensor.matmul(o[:, at + P:at + 2 * P], gv[:, 1, ch],
                                        Sd[:, half, (pair * 2 + 1) * P:(pair * 2 + 2) * P], start=False, stop=True)
            last.then_inc(*S.step("gla out"))
            norm_sums("gn", "gla out squares",
                      [(eq, ek)[c // 4][:, (c % 4) * P:(c % 4 + 1) * P] for c in range(8)])
            norm_rows("gn", [bank[6 + c // 4][:, (c % 4) * P:(c % 4 + 1) * P] for c in range(8)])

            def mix_ready(k):
                kind = "gla mix" if k < 4 else "conv y"
                pe.wait_ge(*done(f"{kind} high {k % 4}"))
                pe.wait_ge(*done(f"{kind} low {k % 4}"))
            for u in range(4):
                unit(FIRST_UNIT["wout"] + u, T, (xh, xl), mix_ready if u == 0 else None)
            for k in range(2):
                pe.wait_ge(*done(f"p high {k}"))
                pe.wait_ge(*done(f"p low {k}"))
            blocks_in_turn(FIRST_UNIT["pproj"], T, lambda b, k: (xh[:, 8 + k, 0:T], xl[:, 8 + k, 0:T]), 2)
            ffn_up(2, T, "f2")
            ffn_down(2, T)
            n = FIRST_UNIT["pgate"]
            unit(n, T, us, u_ready("e"))
            norm_sums("e", "e squares", squares(0, T))
            unit(n + 1, T, us, None, lambda: norm_rows("e", token_rows(R_BANK, T)))
            unit(n + 2, T, us)
            unit(n + 3, T, us)
            norm_sums("out", "out squares", squares(0, T))
            norm_rows("out", token_rows(R_BANK, T))

        @block.scalar
        def _(act):
            S = Steps("scalar", step_sems["scalar"], marks)

            def high(n, i=None, first=None, middle=None):
                cols, U = UNITS[n]["tiles"] * P, UNITS[n]
                at = 16 * (n // 2 + 1)
                act.wait_ge(loaded[n % 2], at if i is None else 16 * i + at)
                if n >= 2:
                    at = through(n - 2)
                    act.wait_ge(products, at if i is None else i * 2 * UNITS[n - 2]["blocks"] + at)
                split = first_half(n) if first else 0
                if first:
                    nc.scalar.activation(wh[n % 2][:, 0:split], raw[n % 2][:, 0:split], ACT.Copy).then_inc(*S.step(first))
                if middle:
                    middle()
                nc.scalar.activation(wh[n % 2][:, split:cols], raw[n % 2][:, split:cols], ACT.Copy).then_inc(high_parts, 1)

            def block_done(b, i=None, stride=0):
                act.wait_ge(products, b + 1 if i is None else i * stride + (b + 1))

            def square(name, c, src, T, sem_and_1, k=None, i=None):
                if i is not None and name != "e":
                    act.wait_ge(*done(f"{name} acc {k}", (i, 1)))
                elif i is not None:
                    pass
                elif c >= 2 and name in LOOPED:
                    act.wait_ge(*done(f"{name} acc {c % 2}", (DC - 4) // 2))
                elif c >= 2:
                    act.wait_ge(*done(f"{name} acc {c - 2}"))
                nc.scalar.activation(sq[:, (c if k is None else k) % 2, 0:T], src, ACT.Square).then_inc(*sem_and_1)

            def u_high(name, c, T, t0, gain, k=None, i=None):
                label = c if k is None else k
                if i is not None:
                    act.wait_ge(*done(f"{name} acc {k}", (i, 1)))
                nc.scalar.activation(uh[:, c, 0:T], h[:, c, t0:t0 + T], ACT.Copy, scale=pcol(gain, c))\
                    .then_inc(*S.step(f"{name} u high {label}"))
                square(name, c, h[:, c, t0:t0 + T], T, S.step(f"{name} sq {label}"), k, i)

            def post(name, c, n, b, gain, k=None, i=None, stride=0, scale=None):
                block_done(b, i, stride)
                nc.scalar.activation(m[:, c, :], bank[BLOCKS[b]["bank"]][:, 0:T1], ACT.Copy, scale=gain)\
                    .then_inc(*S.step())
                if scale is None:
                    square(name, c, bank[BLOCKS[b]["bank"]][:, 0:T1], T1, (freed["a"], 1), k, i)
                else:
                    if c >= 2:
                        act.wait_ge(*done(f"{name} acc {c - 2}"))
                    nc.scalar.activation(sq[:, c % 2, :], bank[BLOCKS[b]["bank"]][:, 0:T1], ACT.Square,
                                         scale=scale).then_inc(freed["a"], 1)

            def ffn_up(l, T, conv):
                n0, b0 = FIRST_UNIT[f"up{l}"], FIRST_BLOCK[f"up{l}"]

                def x_high(turn_, j):
                    k, i = turn_
                    act.wait_ge(*done(f"x full {l} {k}", i))
                    nc.scalar.activation(xh[:, j, 0:T], xf[:, 0:T], ACT.Copy).then_inc(*S.step(f"x high {l} {k}"))

                def turn(j, place, before):
                    k, i = place
                    n = n0 + (j if i is None else 2 + int(k[1]))
                    U = UNITS[n]
                    high(n + 2, i, f"first high {l} {k}", middle=None if conv else lambda: silu(n, i, k))
                    if conv:
                        if before is not None:
                            act.wait_ge(*done(f"x full {l} {k}", i))
                        for hf in range(2):
                            B = BLOCKS[U["first"] + hf]
                            act.wait_ge(freed["v"], B["freed"] if i is None else 4 * i + B["freed"])
                            nc.scalar.activation(cv[:, hf, 0:T], ur[:, hf, 2:2 + T], ACT.Identity,
                                                 bias=pcol(f"cb{l}", hf * FC + j),
                                                 scale=pcol(f"cw{l}", (2 * 2 + hf) * FC + j))\
                                .then_inc(*S.step(f"tap 2 {l} {hf} {k}"))
                        if before is not None:
                            x_high(place, j - 1)
                        act.wait_ge(*done(f"taps {l} 0 {k}", i))
                        nc.scalar.activation(cv[:, 0, 0:T], cv[:, 0, 0:T], ACT.Silu).then_inc(*S.step(f"silu {l} {k}"))
                    else:
                        x_high(place, j)

                def silu(n, i, k):
                    B = BLOCKS[UNITS[n]["first"]]
                    act.wait_ge(freed["v"], B["freed"] if i is None else 4 * i + B["freed"])
                    nc.scalar.activation(cv[:, 0, 0:T], ur[:, 0, 2:2 + T], ACT.Silu).then_inc(*S.step(f"silu {l} {k}"))

                nc.scalar.activation(warm[:, :], ident[:, 0:1], ACT.Silu).then_inc(*S.step())
                up_turns(act, S, l, turn)
                if conv:
                    x_high(up_place(FC), FC - 1)

            def ffn_down(l):
                n0, b0 = FIRST_UNIT[f"down{l}"], FIRST_BLOCK[f"down{l}"]
                with act.Fori(0, (DC - 2) // 2) as i:
                    S.enter(f"down{l}", i)
                    for k in range(2):
                        high(n0 + k + 2, i)
                        post(f"fpost{l}", 2 * i + k, n0 + k, b0 + k, pcol(f"ffn_post{l}", 2 * i + k), k, i, 2)
                    S.leave((DC - 2) // 2)
                for c in range(DC - 2, DC):
                    high(n0 + c + 2)
                    post(f"fpost{l}", c, n0 + c, b0 + c, pcol(f"ffn_post{l}", c))

            high(0)
            act.wait_ge(tables_in, 64)
            for c in range(DC):
                if c % 4 == 0:
                    act.wait_ge(h_in[c // 4], 16)
                u_high("a0", c, T1, 0, "mix_pre0")
                if c == 3:
                    high(1)
            n = FIRST_UNIT["dq"]
            high(n + 2)
            for j in range(QC + KC):
                if j == QC:
                    high(n + 3)
                b = FIRST_BLOCK["dq"] + j
                act.wait_ge(freed["v"], BLOCKS[b]["freed"])
                if j >= 2:
                    act.wait_ge(*done(f"latent acc {j - 2}"))
                nc.scalar.activation(sq[:, j % 2, :], m[:, j, :], ACT.Square).then_inc(*S.step(f"latent sq {j}"))
            high(n + 4)
            act.wait_ge(*done("k rope full"))
            nc.scalar.activation(K[64:96, :, :], kr[64:96, :].unsqueeze(1).to_broadcast([32, NH, T1]), ACT.Copy)\
                .then_inc(*S.step("k rope"))
            for j in range(QC + KC):
                act.wait_ge(*done(f"latent {j}"))
                g = pcol("q_norm", j) if j < QC else pcol("kv_norm", j - QC)
                nc.scalar.activation(uh[:, j, :], m[:, j, :], ACT.Copy, scale=g).then_inc(*S.step(f"c u high {j}"))

            def heads_out(name, dst):
                for b in range(8):
                    block_done(FIRST_BLOCK[name] + b)
                    src = bank[BLOCKS[FIRST_BLOCK[name] + b]["bank"]]
                    nc.scalar.activation(dst[0:64, 2 * b, :], src[0:64, 0:T1], ACT.Copy).then_inc(*S.step())
                    nc.scalar.activation(dst[0:64, 2 * b + 1, :], src[64:128, 0:T1], ACT.Copy)\
                        .then_inc(freed["a"], 1)
            heads_out("uqn", Q)
            high(FIRST_UNIT["uqn"] + 2)
            high(FIRST_UNIT["uqn"] + 3)
            heads_out("uk", K)
            high(FIRST_UNIT["uqn"] + 4)
            high(FIRST_UNIT["uqn"] + 5)
            for s in range(NH + 4):
                if s < NH:
                    act.wait_ge(*done(f"neg max {s}"))
                    if s >= 2:
                        act.wait_ge(*done(f"transposes {s - 2}"))
                    X, Y = bank[s % 2], bank[2 + s % 2]
                    for t, src in enumerate((X[0:96, 0:96], X[0:96, 96:288], Y[0:80, 0:T1])):
                        nq, at, w = QT[t][1], (0, 96, 288)[t], src.shape[1]
                        step = S.step(f"exp {s}")
                        nc.scalar.activation(Pp[0:nq, s % 2, at:at + w], src, ACT.Exp, bias=nb[0:nq, s % 2, t:t + 1],
                                             scale=SCALE, accum_out=sm[0:nq, s % 2, t:t + 1]).then_inc(*step)
                if 2 <= s <= NH + 1:
                    g = s - 2
                    act.wait_ge(*done(f"transposes {g}"))
                    if g >= 2:
                        act.wait_ge(*done(f"values {g - 2}"))
                    nc.scalar.activation(PT[:, g % 2, 0:T1], bank[4][0:96, 0:T1], ACT.Copy)\
                        .then_inc(*S.step(f"transposed a {g}"))
                if s >= 4 and s % 2 == 0:
                    pair = (s - 4) // 2
                    act.wait_ge(*done(f"values {2 * pair + 1}"))
                    nc.scalar.activation(uh[:, pair, :], bank[6 + pair % 2][:, 0:T1], ACT.Copy)\
                        .then_inc(*S.step(f"att out {pair} high"))
            for u in range(4):
                n = FIRST_UNIT["wo"] + u
                high(n + 2)
                for b in range(2):
                    post("post0", 2 * u + b, n, FIRST_BLOCK["wo"] + 2 * u + b, pcol("mix_post0", 2 * u + b))
            for c in range(DC):
                act.wait_ge(*done(f"f0 h {c}"))
                u_high("f0", c, T1, 0, "ffn_pre0")
            ffn_up(0, T1, True)
            ffn_down(0)
            for c in range(DC):
                act.wait_ge(*done(f"a1 h {c}"))
                square("a1", c, h[:, c, :], T1, S.step(f"a1 sq {c}"))
            for g in range(4):
                act.wait_ge(*done(f"pool mixed {g}"))
                nc.scalar.activation(uh[:, 2 * g:2 * g + 2, :], pb[:, 0:2, 16:16 + T1], ACT.Copy)\
                    .then_inc(*S.step(f"pool mixed high {g}"))
            act.wait_ge(*done("pool gains"))
            n = FIRST_UNIT["pool"]
            for b in range(8):
                post("post1", b, n, FIRST_BLOCK["pool"] + b, psg[:, b:b + 1], scale=pcol("pool_scale", b))
            high(n + 2)
            for c in range(DC):
                act.wait_ge(*done(f"f1 h {c}"))
                u_high("f1", c, T1, 0, "ffn_pre1")
            ffn_up(1, T1, True)
            ffn_down(1)
            T = SEQ
            for c in range(DC):
                act.wait_ge(*done(f"g h {c}"))
                u_high("g", c, T, META, "ln1")
            n = FIRST_UNIT["gin_a"]
            high(n + 2)
            high(n + 3)
            act.wait_ge(*done("gate -|x|"))
            nc.scalar.activation(ek[:, :], eq[:, :], ACT.Exp).then_inc(*S.step())
            act.wait_ge(*S.now())
            nc.scalar.activation(ek[:, :], ek[:, :], ACT.Ln, bias=1.0).then_inc(*S.step("gate log"))
            for v in range(2):
                for t in range(2):
                    b = FIRST_BLOCK["gin_v"] + 2 * v + t
                    block_done(b)
                    nc.scalar.activation(gv[:, t, v * 256:(v + 1) * 256], bank[BLOCKS[b]["bank"]][:, 0:256],
                                         ACT.Copy, scale=ny[:, t:t + 1]).then_inc(freed["a"], 1)
                high(n + 4 + v)

            def level_exps(l):
                B = 1 << l
                v = lambda t, side: t[:, :].rearrange("p (n s b) -> p n s b", s=2, b=B)[:, :, side, :]
                act.wait_ge(*done(f"level {l} sums"))
                nc.scalar.activation(v(eq, 1), v(pre, 1), ACT.Exp).then_inc(*S.step(f"level {l} exp q"))
                nc.scalar.activation(v(ek, 0), v(suf, 0), ACT.Exp).then_inc(*S.step(f"level {l} exp k"))

            level_exps(0)
            for v in range(2):
                high(n + 6 + v)
                level_exps(1 + v)
            for j in range(4):
                u = FIRST_UNIT["gin_c"] + j
                act.wait_ge(*done(f"conv in {j}"))
                nc.scalar.activation(cv[:, 0, 0:T], ur[:, 0, 2:2 + T], ACT.Copy, scale=pcol("conv2", 8 + j))\
                    .then_inc(*S.step(f"conv tap 2 {j}"))
                high(u + 2)
                act.wait_ge(*done(f"conv y {j}"))
                nc.scalar.activation(xh[:, 4 + j, 0:T], xf[:, 0:T], ACT.Copy).then_inc(*S.step(f"conv y high {j}"))
                level_exps(3 + j)
            level_exps(7)
            nc.scalar.activation(m[:, 0:4, 0:T], m[:, 0:4, 0:T], ACT.Silu).then_inc(*S.step("gla gate"))
            act.wait_ge(*done("gla out"))
            for pair in range(2):
                src = bank[6 + pair][:, :]
                nc.scalar.activation(m[:, 4 + 2 * pair:6 + 2 * pair, 0:T], src.rearrange("p (a t) -> p a t", a=2),
                                     ACT.Copy).then_inc(*S.step())
                step = S.step("gla out squares")
                nc.scalar.activation((eq, ek)[pair][:, :], src, ACT.Square).then_inc(*step)
            for head in range(GH):
                act.wait_ge(*done(f"gla mix {head}"))
                nc.scalar.activation(xh[:, head, 0:T], m[:, 4 + head, 0:T], ACT.Copy)\
                    .then_inc(*S.step(f"gla mix high {head}"))
            act.wait_ge(p_in, 16)
            for k in range(2):
                nc.scalar.activation(xh[:, 8 + k, 0:T], cv[:, k, 0:T], ACT.Copy).then_inc(*S.step(f"p high {k}"))
            for u in range(4):
                n = FIRST_UNIT["wout"] + u
                high(n + 2)
                for c in range(2 * u, 2 * u + 2):
                    act.wait_ge(freed["v"], BLOCKS[FIRST_BLOCK["wout"] + c]["freed"])
                    u_high("f2", c, T, META, "ln2")
            for b in range(8):
                block_done(FIRST_BLOCK["pproj"] + b)
                nc.scalar.activation(m[:, b, 0:T], bank[BLOCKS[FIRST_BLOCK["pproj"] + b]["bank"]][:, 0:T], ACT.Copy)\
                    .then_inc(freed["a"], 1)
            high(FIRST_UNIT["pproj"] + 2)
            ffn_up(2, T, False)
            n0, b0 = FIRST_UNIT["down2"], FIRST_BLOCK["down2"]
            with act.Fori(0, (DC - 2) // 2) as i:
                S.enter("down2", i)
                for k in range(2):
                    high(n0 + k + 2, i)
                    act.wait_ge(freed["v"], 2 * i + BLOCKS[b0 + k]["freed"])
                    u_high("e", 2 * i + k, T, META, "ln3", k, i)
                S.leave((DC - 2) // 2)
            for c in range(DC - 2, DC):
                high(n0 + c + 2)
                act.wait_ge(freed["v"], BLOCKS[b0 + c]["freed"])
                u_high("e", c, T, META, "ln3")
            for u in range(4):
                n = FIRST_UNIT["pgate"] + u
                for b in range(2):
                    c = 2 * u + b
                    act.wait_ge(freed["v"], BLOCKS[FIRST_BLOCK["pgate"] + c]["freed"])
                    nc.scalar.activation(cv[:, b, 0:T], cv[:, b, 0:T], ACT.Sigmoid).then_inc(*S.step(f"ple gate {c}"))
                if n + 2 < len(UNITS):
                    high(n + 2)
                for c in range(2 * u, 2 * u + 2):
                    act.wait_ge(*done(f"out h {c}"))
                    square("out", c, h[:, c, META:T1], T, S.step(f"out sq {c}"))

        @block.vector
        def _(dve):
            S = Steps("vector", step_sems["vector"], marks)

            def low(n, i=None, first=None, middle=None):
                cols, split = vector_cols(n), 0
                if first:
                    split = first_half(n)
                    dve.wait_ge(*done(first, i))
                    nc.vector.tensor_tensor(wl[n % 2][:, 0:split], raw[n % 2][:, 0:split],
                                            wh[n % 2][:, 0:split].bitcast(F32), ALU.subtract).then_inc(*S.step())
                if middle:
                    middle()
                dve.wait_ge(high_parts, n + 1 if i is None else 2 * i + (n + 1))
                nc.vector.tensor_tensor(wl[n % 2][:, split:cols], raw[n % 2][:, split:cols],
                                        wh[n % 2][:, split:cols].bitcast(F32), ALU.subtract).then_inc(low_parts_v, 1)

            def block_done(b, i=None, stride=0):
                dve.wait_ge(products, b + 1 if i is None else i * stride + (b + 1))

            def u_low(name, c, T, t0, gain, k=None, i=None):
                label = c if k is None else k
                dve.wait_ge(*done(f"{name} u high {label}", i))
                nc.vector.scalar_tensor_tensor(ul[:, c, 0:T], h[:, c, t0:t0 + T], pcol(gain, c),
                                               uh[:, c, 0:T].bitcast(F32), ALU.mult, ALU.subtract)\
                    .then_inc(*S.step(f"{name} u low {label}"))

            def norm(name, slices):
                n = slices[-1][1]
                dve.wait_ge(*done(f"{name} sums"))
                for c0, c1, inv in slices:
                    nc.vector.tensor_scalar(nx[:, c0:c1], bank[NORM_BANK][:, c0:c1], inv, EPS, ALU.mult, ALU.add)\
                        .then_inc(*S.step())
                dve.wait_ge(*S.now())
                x, half, t, y = nx[:, 0:n], nh[:, 0:n], nt[:, 0:n], ny[:, 0:n]
                nc.vector.tensor_scalar(t.bitcast(I32), x.bitcast(I32), 1, None, ALU.arith_shift_right)\
                    .then_inc(*S.step())
                nc.vector.tensor_scalar(half, x, -0.5, None, ALU.mult).then_inc(*S.step())
                dve.wait_ge(*S.now())
                nc.vector.tensor_scalar(y.bitcast(I32), t.bitcast(I32), -1.0, float(0x5F3759DF), ALU.mult, ALU.add)\
                    .then_inc(*S.step())
                for _ in range(3):
                    dve.wait_ge(*S.now())
                    nc.vector.tensor_tensor(t, y, y, ALU.mult).then_inc(*S.step())
                    dve.wait_ge(*S.now())
                    nc.vector.tensor_tensor(t, t, half, ALU.mult).then_inc(*S.step())
                    dve.wait_ge(*S.now())
                    nc.vector.scalar_tensor_tensor(y, t, 1.5, y, ALU.add, ALU.mult).then_inc(*S.step())
                dve.wait_ge(*S.now())
                for c in range(n):
                    step = S.step(f"{name} diagonal")
                    nc.vector.tensor_scalar(diag[:, c * P:(c + 1) * P], ident[:, :], ny[:, c:c + 1], None, ALU.mult)\
                        .then_inc(*step)

            def one(T, a=0):
                return [(a, a + -(-T // P), 1.0 / D)]

            def keep_rows(name, T):
                dve.wait_ge(*done(f"{name} rows"))
                nc.vector.tensor_copy(rows[:, 0:T], bank[R_BANK][:, 0:T]).then_inc(*S.step())
                dve.wait_ge(*S.now())

            def scaled(out, b, sem_and_1, T, i=None, stride=0):
                block_done(b, i, stride)
                nc.vector.tensor_tensor(out, bank[BLOCKS[b]["bank"]][:, 0:T], rows[:, 0:T], ALU.mult)\
                    .then_inc(*sem_and_1)

            def freed_wait(b, i=None):
                dve.wait_ge(freed["v"], BLOCKS[b]["freed"] if i is None else 4 * i + BLOCKS[b]["freed"])

            def add_post(name, nxt, gain, T, t0):
                norm(name, one(T1))
                dve.wait_ge(*done(f"{name} rows"))
                for c in range(DC + 1):
                    if c < DC:
                        nc.vector.tensor_tensor(m[:, c, :], m[:, c, :], bank[R_BANK][:, 0:T1], ALU.mult)\
                            .then_inc(*S.step())
                        dve.wait_ge(*S.now())
                        nc.vector.tensor_tensor(h[:, c, :], h[:, c, :], m[:, c, :], ALU.add)\
                            .then_inc(*S.step(f"{nxt} h {c}"))
                    if c >= 1 and gain is not None:
                        u_low(nxt, c - 1, T, t0, gain)

            def ffn_up(l, T, conv, name):
                n0 = FIRST_UNIT[f"up{l}"]
                norm(name, one(T))
                keep_rows(name, T)

                def x_full(place, of):
                    k, i = place
                    dve.wait_ge(*done(f"silu {l} {of[0]}", of[1]))
                    dve.wait_ge(*S.now())
                    value = cv[:, 1, 0:T] if conv else ur[:, 1, 2:2 + T]
                    nc.vector.tensor_tensor(xf[:, 0:T], cv[:, 0, 0:T], value, ALU.mult)\
                        .then_inc(*S.step(f"x full {l} {k}"))

                def x_low(place, j):
                    k, i = place
                    dve.wait_ge(*done(f"x high {l} {k}", i))
                    nc.vector.tensor_tensor(xl[:, j, 0:T], xf[:, 0:T], xh[:, j, 0:T].bitcast(F32), ALU.subtract)\
                        .then_inc(*S.step(f"x low {l} {k}"))

                def turn(j, place, before):
                    k, i = place
                    n = n0 + (j if i is None else 2 + int(k[1]))
                    b = UNITS[n]["first"]
                    dve.wait_ge(*S.now())
                    scaled(ur[:, 0, 2:2 + T], b, (freed["v"], 1), T, i, 4)
                    scaled(ur[:, 1, 2:2 + T], b + 1, (freed["v"], 1), T, i, 4)
                    if conv:
                        if before is not None:
                            x_full(place, before)
                        low(n + 2, i, f"first high {l} {k}")
                        for tap in (1, 0):
                            for hf in range(2):
                                if tap == 1:
                                    dve.wait_ge(*done(f"tap 2 {l} {hf} {k}", i))
                                elif hf == 0:
                                    dve.wait_ge(*S.now())
                                nc.vector.scalar_tensor_tensor(
                                    cv[:, hf, 0:T], ur[:, hf, tap:tap + T], pcol(f"cw{l}", (tap * 2 + hf) * FC + j),
                                    cv[:, hf, 0:T], ALU.mult, ALU.add).then_inc(*S.step(f"taps {l} {hf} {k}"))
                        if before is not None:
                            x_low(place, j - 1)
                    else:
                        def full():
                            freed_wait(b + 1, i)
                            x_full(place, place)
                        low(n + 2, i, f"first high {l} {k}", full)
                        x_low(place, j)

                up_turns(dve, S, l, turn)
                if conv:
                    x_full(up_place(FC), up_place(FC - 1))
                    x_low(up_place(FC), FC - 1)

            def ffn_down_lows(l):
                n0 = FIRST_UNIT[f"down{l}"]
                with dve.Fori(0, (DC - 2) // 2) as i:
                    for k in range(2):
                        low(n0 + k + 2, i)
                for c in range(DC - 2, DC):
                    low(n0 + c + 2)

            nc.vector.memset(ones[:, :], 1.0).then_inc(*S.step())
            nc.vector.memset(ur[:, :, :], 0.0).then_inc(*S.step())
            nc.vector.memset(mx[:, :, :], 0.0).then_inc(*S.step())
            nc.vector.memset(sm[:, :, :], 1.0).then_inc(*S.step())
            nc.vector.memset(acc[:, :, :], 0.0).then_inc(*S.step("constants"))
            low(0)
            for c in range(DC):
                u_low("a0", c, T1, 0, "mix_pre0")
                if c == 3:
                    low(1)
            low(2)
            nc.vector.tensor_tensor(psg[:, :], pcol("pool_scale", 0, 8), pcol("mix_post1", 0, 8), ALU.mult)\
                .then_inc(*S.step("pool gains"))
            norm("a0", one(T1))
            keep_rows("a0", T1)
            for hf in range(2):
                nc.vector.tensor_tensor(ropeR[:, hf, :], rope[:, hf, :], rows[:, :], ALU.mult).then_inc(*S.step())
            for j in range(QC + KC):
                if j == QC:
                    low(3)
                scaled(m[:, j, :], FIRST_BLOCK["dq"] + j, (freed["v"], 1), T1)
            b = FIRST_BLOCK["dkr"]
            dve.wait_ge(*S.now())
            for hf, dst in ((0, kr), (1, rb)):
                block_done(b + hf)
                nc.vector.tensor_tensor(dst[:, :], bank[BLOCKS[b + hf]["bank"]][:, 0:T1], ropeR[:, hf, :], ALU.mult)\
                    .then_inc(freed["v"], 1)
            freed_wait(b + 1)
            nc.vector.tensor_tensor(kr[:, :], kr[:, :], rb[:, :], ALU.add).then_inc(*S.step("k rope full"))
            low(4)
            norm("c", [(0, 3, 1.0 / QR), (3, 6, 1.0 / KVR)])
            dve.wait_ge(*done("c rows"))
            for j in range(QC + KC + 1):
                if j < QC + KC:
                    r = bank[R_BANK][:, 0:T1] if j < QC else bank[NORM_BANK][:, P:P + T1]
                    nc.vector.tensor_tensor(m[:, j, :], m[:, j, :], r, ALU.mult).then_inc(*S.step(f"latent {j}"))
                if j >= 1:
                    c = j - 1
                    dve.wait_ge(*done(f"c u high {c}"))
                    g = pcol("q_norm", c) if c < QC else pcol("kv_norm", c - QC)
                    nc.vector.scalar_tensor_tensor(ul[:, c, :], m[:, c, :], g, uh[:, c, :].bitcast(F32),
                                                   ALU.mult, ALU.subtract).then_inc(*S.step(f"c u low {c}"))
            low(5)
            for q4 in range(4):
                b = FIRST_BLOCK["uqr"] + 2 * q4
                for hf, dst in ((0, ra), (1, rb)):
                    block_done(b + hf)
                    if hf == 0:
                        dve.wait_ge(*S.now())
                    nc.vector.tensor_tensor(dst[:, :], bank[BLOCKS[b + hf]["bank"]][:, 0:T1], rope[:, hf, :], ALU.mult)\
                        .then_inc(freed["v"], 1)
                freed_wait(b + 1)
                for j in range(4):
                    part = slice(32 * j, 32 * j + 32)
                    nc.vector.tensor_tensor(Q[64:96, 4 * q4 + j, :], ra[part, :], rb[part, :], ALU.add)\
                        .then_inc(*S.step())
            low(6)
            for half in range(2):
                for t, (q0, nq) in enumerate(QT):
                    if half == 1 and t == 0:
                        low(7)
                    b = FIRST_BLOCK["uv"] + half * 3 + t
                    block_done(b)
                    nc.vector.tensor_copy(V[0:nq, t, half * 512:(half + 1) * 512], bank[BLOCKS[b]["bank"]][0:nq, :])\
                        .then_inc(freed["v"], 1)
            low(8)
            for s in range(NH + 4):
                if s < NH:
                    X, Y, p = bank[s % 2], bank[2 + s % 2], s % 2
                    dve.wait_ge(*done(f"scores {s}"))
                    dv = X[0:96, 0:384].rearrange("q (a b) -> q a b", a=2)[:, :, 0:96]
                    nc.vector.tensor_tensor(dv, dv, cmask[:, :].unsqueeze(1).to_broadcast([96, 2, 96]), ALU.add)\
                        .then_inc(*S.step())
                    nc.vector.tensor_tensor(Y[0:80, 192:T1], Y[0:80, 192:T1], cmask[0:80, 0:80], ALU.add)\
                        .then_inc(*S.step())
                    dve.wait_ge(*S.now())
                    for t, src in enumerate((X[0:96, 0:96], X[0:96, 96:288], Y[0:80, 0:T1])):
                        nc.vector.reduce_max(mx[0:QT[t][1], p, t:t + 1], src, AX).then_inc(*S.step())
                    dve.wait_ge(*S.now())
                    nc.vector.tensor_scalar(nb[:, p, :], mx[:, p, :], -SCALE, None, ALU.mult)\
                        .then_inc(*S.step(f"neg max {s}"))
                if 1 <= s <= NH:
                    g, p = s - 1, (s - 1) % 2
                    dve.wait_ge(*done(f"exp {g}"))
                    nc.vector.reciprocal(rc[:, p, :], sm[:, p, :]).then_inc(*S.step())
                    dve.wait_ge(*S.now())
                    for t, w in enumerate((96, 192, T1)):
                        nq, at = QT[t][1], (0, 96, 288)[t]
                        step = S.step(f"probs {g}")
                        nc.vector.tensor_scalar(Pp[0:nq, p, at:at + w], Pp[0:nq, p, at:at + w], rc[0:nq, p, t:t + 1],
                                                None, ALU.mult).then_inc(*step)
                if 2 <= s <= NH + 1:
                    g = s - 2
                    dve.wait_ge(*done(f"transposes {g}"))
                    if g >= 2:
                        dve.wait_ge(*done(f"values {g - 2}"))
                    nc.vector.tensor_copy(PT[0:96, g % 2, T1:T1 + 176], bank[5][0:96, 0:176]).then_inc(*S.step())
                    nc.vector.tensor_copy(PT[0:80, g % 2, 448:528], bank[5][0:80, 176:256])\
                        .then_inc(*S.step(f"transposed b {g}"))
                if s >= 4 and s % 2 == 0:
                    pair = (s - 4) // 2
                    dve.wait_ge(*done(f"att out {pair} high"))
                    nc.vector.tensor_tensor(ul[:, pair, :], bank[6 + pair % 2][:, 0:T1], uh[:, pair, :].bitcast(F32),
                                            ALU.subtract).then_inc(*S.step(f"att out {pair} low"))
            for u in range(4):
                low(FIRST_UNIT["wo"] + u + 2)
            add_post("post0", "f0", "ffn_pre0", T1, 0)
            ffn_up(0, T1, True, "f0")
            ffn_down_lows(0)
            add_post("fpost0", "a1", None, T1, 0)

            nc.vector.memset(pa[:, :, 0:16], 0.0).then_inc(*S.step())
            nc.vector.memset(pb[:, :, 0:16], 0.0).then_inc(*S.step())
            dve.wait_ge(tables_in, 80)
            norm("a1", one(T1))
            dve.wait_ge(*done("a1 rows"))
            for g in range(4):
                ping, pong = pb[:, 0:2, :], pb[:, 2:4, :]
                a = pa[:, 2 * (g % 2):2 * (g % 2) + 2, :]
                nc.vector.tensor_tensor(a[:, :, 16:16 + T1], h[:, 2 * g:2 * g + 2, :],
                                        bank[R_BANK][:, 0:T1].unsqueeze(1).to_broadcast([P, 2, T1]), ALU.mult)\
                    .then_inc(*S.step())
                dve.wait_ge(*S.now())
                for c in range(2):
                    nc.vector.tensor_scalar(a[:, c, 16:16 + T1], a[:, c, 16:16 + T1], pcol("mix_pre1", 2 * g + c), None,
                                            ALU.mult).then_inc(*S.step())
                dve.wait_ge(*S.now())
                src, dst = a, (ping if g % 2 else pong)
                for d in range(g + 1):
                    w = 1 << d
                    nc.vector.tensor_tensor(dst[:, :, 16:16 + T1], src[:, :, 16:16 + T1], src[:, :, 16 - w:16 + T1 - w],
                                            ALU.add).then_inc(*S.step())
                    dve.wait_ge(*S.now())
                    src, dst = dst, (pong if dst is ping else ping)
                other = ping if src is pong else pong
                nc.vector.tensor_tensor(pong[:, :, 16:16 + T1], src[:, :, 16:16 + T1],
                                        icnt[:, g, :].unsqueeze(1).to_broadcast([P, 2, T1]), ALU.mult)\
                    .then_inc(*S.step())
                dve.wait_ge(*S.now())
                nc.vector.tensor_tensor(ping[:, :, 16:16 + T1], pong[:, :, 16:16 + T1], a[:, :, 16:16 + T1], ALU.subtract)\
                    .then_inc(*S.step(f"pool mixed {g}"))
                dve.wait_ge(*done(f"pool mixed high {g}"))
                nc.vector.tensor_tensor(ul[:, 2 * g:2 * g + 2, :], ping[:, :, 16:16 + T1],
                                        uh[:, 2 * g:2 * g + 2, :].bitcast(F32), ALU.subtract)\
                    .then_inc(*S.step(f"pool mixed low {g}"))
                dve.wait_ge(*S.now())
            low(FIRST_UNIT["pool"] + 2)
            add_post("post1", "f1", "ffn_pre1", T1, 0)
            ffn_up(1, T1, True, "f1")
            ffn_down_lows(1)
            T = SEQ
            add_post("fpost1", "g", "ln1", T, META)

            norm("g", one(T))
            keep_rows("g", T)
            n, b = FIRST_UNIT["gin_a"], FIRST_BLOCK["gin_a"]
            scaled(glr[:, :], b, (freed["v"], 1), T)
            for pair in range(2):
                block_done(b + 1 + pair)
                nc.vector.scalar_tensor_tensor(gq[:, pair * T:(pair + 1) * T], bank[BLOCKS[b + 1 + pair]["bank"]][:, 0:T],
                                               float(GDK) ** -0.5, rows[:, 0:T], ALU.mult, ALU.mult)\
                    .then_inc(freed["v"], 1)
            low(n + 2)
            for pair in range(2):
                scaled(gk[:, pair * T:(pair + 1) * T], FIRST_BLOCK["gin_k"] + pair, (freed["v"], 1), T)
            low(n + 3)
            dve.wait_ge(*done("gate logits"))
            for pair in range(2):
                nc.vector.tensor_scalar(pre[:, pair * T:(pair + 1) * T], bank[6][:, pair * T:(pair + 1) * T],
                                        pcol("b_gate", pair), None, ALU.add).then_inc(*S.step())
            dve.wait_ge(*S.now())
            nc.vector.scalar_tensor_tensor(eq[:, :], pre[:, :], -1.0, pre[:, :], ALU.mult, ALU.min)\
                .then_inc(*S.step("gate -|x|"))
            for t in (suf, ql, kl):
                nc.vector.memset(t[:, :], 0.0).then_inc(*S.step())
            nc.vector.memset(Sd[:, :, :], 0.0).then_inc(*S.step("gate inputs"))
            dve.wait_ge(*done("gate log"))
            nc.vector.scalar_tensor_tensor(pre[:, :], pre[:, :], 0.0, ek[:, :], ALU.min, ALU.subtract)\
                .then_inc(*S.step())
            dve.wait_ge(*S.now())
            nc.vector.tensor_scalar(pre[:, :], pre[:, :], 1.0 / 16.0, None, ALU.mult).then_inc(*S.step("level 0 sums"))
            for v in range(2):
                low(n + 4 + v)

            def level_operands(l):
                B = 1 << l
                v = lambda t, side: t[:, :].rearrange("p (n s b) -> p n s b", s=2, b=B)[:, :, side, :]
                if l > 0:
                    dve.wait_ge(*done(f"level {LEVEL_BEFORE[l]} scores"))
                dve.wait_ge(*done(f"level {l} exp q"))
                nc.vector.tensor_tensor(v(ql, 1), v(gq, 1), v(eq, 1), ALU.mult).then_inc(*S.step(f"level {l} q"))
                dve.wait_ge(*done(f"level {l} exp k"))
                nc.vector.tensor_tensor(v(kl, 0), v(gk, 0), v(ek, 0), ALU.mult).then_inc(*S.step(f"level {l} k"))
                if l < FAR:
                    nb_ = 2 * SEQ // (2 * B)
                    total = lambda side: v(pre, side)[:, :, B - 1:B].to_broadcast([P, nb_, B])
                    nc.vector.tensor_tensor(v(suf, 0), v(suf, 0), total(1), ALU.add).then_inc(*S.step())
                    dve.wait_ge(*S.now())
                    nc.vector.tensor_tensor(v(pre, 1), v(pre, 1), total(0), ALU.add)\
                        .then_inc(*S.step(f"level {l + 1} sums"))

            def level_kept(l):
                dve.wait_ge(*done(f"level {l} scores"))
                if l == DIAGONAL:
                    dve.wait_ge(*S.now())
                    dve.wait_ge(tables_in, 16 * 7)
                for half in range(2):
                    if l == FAR:
                        nc.vector.tensor_copy(S01[:, half, :], bank[6 + half][:, 0:2 * P]).then_inc(*S.step(f"level {l} kept {half}"))
                    else:
                        mask = lmask[:, min(l, 7), :].unsqueeze(1).to_broadcast([P, 4, P])
                        nc.vector.copy_predicated(Sd[:, half, :].rearrange("p (a t) -> p a t", a=4), mask,
                                                  bank[6 + half][:, :].rearrange("p (a t) -> p a t", a=4))\
                            .then_inc(*S.step(f"level {l} kept {half}"))
                dve.wait_ge(*S.now())

            level_kept(DIAGONAL)
            level_operands(0)
            for v in range(2):
                for c in range(2):
                    scaled(m[:, 2 * v + c, 0:T], FIRST_BLOCK["gin_g"] + 2 * v + c, (freed["v"], 1), T)
                low(n + 6 + v)
                level_kept(v)
                level_operands(1 + v)
            for j in range(4):
                b = FIRST_BLOCK["gin_c"] + 3 * j
                scaled(ur[:, 0, 2:2 + T], b, (freed["v"], 1), T)
                scaled(ur[:, 1, 2:2 + T], b + 1, (freed["v"], 1), T)
                scaled(xf[:, 0:T], b + 2, (freed["v"], 1), T)
                freed_wait(b + 1)
                nc.vector.tensor_tensor(ur[:, 0, 2:2 + T], ur[:, 0, 2:2 + T], ur[:, 1, 2:2 + T], ALU.mult)\
                    .then_inc(*S.step(f"conv in {j}"))
                low(FIRST_UNIT["gin_c"] + j + 2)
                dve.wait_ge(*done(f"conv tap 2 {j}"))
                for tap in (1, 0):
                    nc.vector.scalar_tensor_tensor(cv[:, 0, 0:T], ur[:, 0, tap:tap + T], pcol("conv2", 4 * tap + j),
                                                   cv[:, 0, 0:T], ALU.mult, ALU.add).then_inc(*S.step())
                    dve.wait_ge(*S.now())
                freed_wait(b + 2)
                nc.vector.tensor_tensor(xf[:, 0:T], xf[:, 0:T], cv[:, 0, 0:T], ALU.mult).then_inc(*S.step(f"conv y {j}"))
                dve.wait_ge(*done(f"conv y high {j}"))
                nc.vector.tensor_tensor(xl[:, 4 + j, 0:T], xf[:, 0:T], xh[:, 4 + j, 0:T].bitcast(F32), ALU.subtract)\
                    .then_inc(*S.step(f"conv y low {j}"))
                dve.wait_ge(*S.now())
                level_kept(2 + j)
                level_operands(3 + j)
            level_kept(6)
            level_operands(7)
            level_kept(7)
            norm("gn", [(0, 8, 1.0 / GDV)])
            dve.wait_ge(*done("gn rows"))
            for pair in range(2):
                o = m[:, 4 + 2 * pair:6 + 2 * pair, 0:T]
                nc.vector.tensor_tensor(o, o, bank[6 + pair][:, :].rearrange("p (a t) -> p a t", a=2), ALU.mult)\
                    .then_inc(*S.step())
            dve.wait_ge(*done("gla gate"))
            dve.wait_ge(*S.now())
            for head in range(GH):
                o = m[:, 4 + head, 0:T]
                nc.vector.scalar_tensor_tensor(o, o, pcol("gn"), m[:, head, 0:T], ALU.mult, ALU.mult)\
                    .then_inc(*S.step(f"gla mix {head}"))
            for head in range(GH):
                dve.wait_ge(*done(f"gla mix high {head}"))
                nc.vector.tensor_tensor(xl[:, head, 0:T], m[:, 4 + head, 0:T], xh[:, head, 0:T].bitcast(F32),
                                        ALU.subtract).then_inc(*S.step(f"gla mix low {head}"))
            for k in range(2):
                dve.wait_ge(*done(f"p high {k}"))
                nc.vector.tensor_tensor(xl[:, 8 + k, 0:T], cv[:, k, 0:T], xh[:, 8 + k, 0:T].bitcast(F32), ALU.subtract)\
                    .then_inc(*S.step(f"p low {k}"))

            def add_block(c, b, i=None, stride=0):
                block_done(b, i, stride)
                nc.vector.tensor_tensor(h[:, c, META:T1], h[:, c, META:T1], bank[BLOCKS[b]["bank"]][:, 0:T], ALU.add)\
                    .then_inc(freed["v"], 1)

            for u in range(4):
                for c in range(2 * u, 2 * u + 2):
                    add_block(c, FIRST_BLOCK["wout"] + c)
                low(FIRST_UNIT["wout"] + u + 2)
                for c in range(2 * u, 2 * u + 2):
                    u_low("f2", c, T, META, "ln2")
            low(FIRST_UNIT["pproj"] + 2)
            ffn_up(2, T, False, "f2")
            n0, b0 = FIRST_UNIT["down2"], FIRST_BLOCK["down2"]
            with dve.Fori(0, (DC - 2) // 2) as i:
                S.enter("down2", i)
                for k in range(2):
                    add_block(2 * i + k, b0 + k, i, 2)
                    low(n0 + k + 2, i)
                    u_low("e", 2 * i + k, T, META, "ln3", k, i)
                S.leave((DC - 2) // 2)
            for c in range(DC - 2, DC):
                add_block(c, b0 + c)
                low(n0 + c + 2)
                u_low("e", c, T, META, "ln3")
            norm("e", one(T))
            keep_rows("e", T)
            for u in range(4):
                n = FIRST_UNIT["pgate"] + u
                for b in range(2):
                    scaled(cv[:, b, 0:T], FIRST_BLOCK["pgate"] + 2 * u + b, (freed["v"], 1), T)
                if n + 2 < len(UNITS):
                    low(n + 2)
                for b in range(2):
                    c = 2 * u + b
                    dve.wait_ge(*done(f"ple gate {c}"))
                    nc.vector.tensor_tensor(cv[:, b, 0:T], cv[:, b, 0:T], m[:, c, 0:T], ALU.mult).then_inc(*S.step())
                    dve.wait_ge(*S.now())
                    nc.vector.tensor_tensor(h[:, c, META:T1], h[:, c, META:T1], cv[:, b, 0:T], ALU.add)\
                        .then_inc(*S.step(f"out h {c}"))
                dve.wait_ge(*S.now())
            norm("out", one(T))
            dve.wait_ge(*done("out rows"))
            for c in range(DC):
                nc.vector.scalar_tensor_tensor(m[:, c, 0:T], h[:, c, META:T1], pcol("lnf", c), bank[R_BANK][:, 0:T],
                                               ALU.mult, ALU.mult).then_inc(*S.step(f"final {c}"))

        @block.gpsimd
        def _(pool):
            S = Steps("pool", step_sems["pool"], marks)

            def low(n, i=None):
                at = slice(vector_cols(n), UNITS[n]["tiles"] * P)
                pool.wait_ge(high_parts, n + 1 if i is None else 2 * i + (n + 1))
                nc.gpsimd.tensor_tensor(wl[n % 2][:, at], raw[n % 2][:, at], wh[n % 2][:, at].bitcast(F32),
                                        ALU.subtract).then_inc(low_parts_g, 1)

            def clear(after, T=T1):
                pool.wait_ge(*done(f"{after} sums"))
                nc.gpsimd.memset(acc[:, 0, 0:T], 0.0).then_inc(*S.step())

            def add_square(name, c, T, ready, a=0, k=None, last=DC - 1):
                label = c if k is None else k
                pool.wait_ge(*ready)
                pool.wait_ge(*S.now())
                step = S.step(f"{name} squares" if k is None and c == last else f"{name} acc {label}")
                nc.gpsimd.tensor_tensor(acc[:, a, 0:T], acc[:, a, 0:T], sq[:, label % 2, 0:T], ALU.add).then_inc(*step)

            def evac(b, i=None, stride=0):
                return freed["a"], (BLOCKS[b]["freed"] if i is None else i * stride + BLOCKS[b]["freed"])

            def up_lows(l):
                n0 = FIRST_UNIT[f"up{l}"]
                with pool.Fori(0, (FC - 2) // 2) as i:
                    for k in range(2):
                        low(n0 + k + 2, i)
                for j in range(FC - 2, FC):
                    low(n0 + j + 2)

            def down(l):
                n0, b0, name = FIRST_UNIT[f"down{l}"], FIRST_BLOCK[f"down{l}"], f"fpost{l}"
                with pool.Fori(0, (DC - 2) // 2) as i:
                    S.enter(f"down{l}", i)
                    for k in range(2):
                        low(n0 + k + 2, i)
                        add_square(name, 2 * i + k, T1, evac(b0 + k, i, 2), k=k)
                    S.leave((DC - 2) // 2)
                for c in range(DC - 2, DC):
                    low(n0 + c + 2)
                    add_square(name, c, T1, evac(b0 + c))

            pool.wait_ge(*done("constants"))
            low(0)
            for c in range(DC):
                add_square("a0", c, T1, done(f"a0 sq {c}"))
                if c == 3:
                    low(1)
            low(2)
            clear("a0")
            for j in range(QC + KC):
                if j == QC:
                    low(3)
                pool.wait_ge(*done(f"latent sq {j}"))
                pool.wait_ge(*S.now())
                step = S.step("kv squares" if j == QC + KC - 1 else f"latent acc {j}")
                a = 0 if j < QC else 1
                nc.gpsimd.tensor_tensor(acc[:, a, 0:T1], acc[:, a, 0:T1], sq[:, j % 2, 0:T1], ALU.add).then_inc(*step)
            for n in range(4, 9):
                low(n)
            clear("c")
            for u in range(4):
                low(FIRST_UNIT["wo"] + u + 2)
                for c in range(2 * u, 2 * u + 2):
                    add_square("post0", c, T1, evac(FIRST_BLOCK["wo"] + c))
            clear("post0")
            for c in range(DC):
                add_square("f0", c, T1, done(f"f0 sq {c}"))
            up_lows(0)
            clear("f0")
            down(0)
            clear("fpost0")
            for c in range(DC):
                add_square("a1", c, T1, done(f"a1 sq {c}"))
            clear("a1")
            for b in range(8):
                add_square("post1", b, T1, evac(FIRST_BLOCK["pool"] + b))
            low(FIRST_UNIT["pool"] + 2)
            clear("post1")
            for c in range(DC):
                add_square("f1", c, T1, done(f"f1 sq {c}"))
            up_lows(1)
            clear("f1")
            down(1)
            T = SEQ
            clear("fpost1")
            for c in range(DC):
                add_square("g", c, T, done(f"g sq {c}"))
            for n in range(FIRST_UNIT["gin_a"] + 2, FIRST_UNIT["gin_c"] + 6):
                low(n)
            clear("g")
            for u in range(4):
                low(FIRST_UNIT["wout"] + u + 2)
                for c in range(2 * u, 2 * u + 2):
                    add_square("f2", c, T, done(f"f2 sq {c}"))
            low(FIRST_UNIT["pproj"] + 2)
            up_lows(2)
            clear("f2")
            n0 = FIRST_UNIT["down2"]
            with pool.Fori(0, (DC - 2) // 2) as i:
                S.enter("down2", i)
                for k in range(2):
                    low(n0 + k + 2, i)
                    add_square("e", 2 * i + k, T, done(f"e sq {k}", i), k=k)
                S.leave((DC - 2) // 2)
            for c in range(DC - 2, DC):
                low(n0 + c + 2)
                add_square("e", c, T, done(f"e sq {c}"))
            low(FIRST_UNIT["pgate"] + 2)
            low(FIRST_UNIT["pgate"] + 3)
            clear("e")
            for c in range(DC):
                add_square("out", c, T, done(f"out sq {c}"))


def _tiles(w, nb, order="kb"):
    kc, units = w.shape[0] // P, w.shape[1] // (nb * P)
    return np.ascontiguousarray(w.reshape(kc, P, units, nb * P).transpose(2, 1, 0, 3)).reshape(units, P, kc * nb * P)


def _columns(v):
    return np.ascontiguousarray(v.reshape(-1, P).T)


def _layout(x):
    f = lambda name: np.asarray(x[name])
    a = {}
    h0 = np.concatenate([f("meta_tokens"), f("x")[0]], axis=0)
    a["h0"] = np.ascontiguousarray(h0.T.reshape(DC, P, T1).transpose(1, 0, 2))
    a["p_t"] = np.ascontiguousarray(f("p_2")[0, 0].T.reshape(2, P, SEQ).transpose(1, 0, 2))
    a["wgu"] = f("w_gate_up_2")[0]
    dqkv = f("mla_w_dqkv")[0]
    a["w_dq"] = _tiles(dqkv[:, 0:QR], 3)
    a["w_dkv"] = _tiles(dqkv[:, QR:QR + KVR], 2)
    krope = np.arange(QR + KVR, QR + KVR + ROPE)
    swap = np.r_[ROPE // 2:ROPE, 0:ROPE // 2]
    a["w_dkr"] = _tiles(dqkv[:, np.r_[np.tile(krope, 4), np.tile(krope[swap], 4)]], 2)
    uq = f("mla_w_uq")[0]
    qd = NOPE + ROPE
    a["w_uqn"] = _tiles(uq[:, np.concatenate([np.arange(NOPE) + i * qd for i in range(NH)])], 8)
    cols = []
    for q4 in range(4):
        for part in (np.arange(ROPE), swap):
            cols += [NOPE + part + i * qd for i in range(4 * q4, 4 * q4 + 4)]
    a["w_uqr"] = _tiles(uq[:, np.concatenate(cols)], 8)
    ukv = f("mla_w_ukv")[0]
    a["w_uk"] = _tiles(ukv[:, np.concatenate([np.arange(NOPE) + i * (NOPE + VD) for i in range(NH)])], 8)
    a["w_uv"] = _tiles(ukv[:, np.concatenate([NOPE + np.arange(VD) + i * (NOPE + VD) for i in range(NH)])], 8)
    a["w_wo"] = _tiles(f("mla_w_o")[0], 2)
    pw = f("pool_w_group")[0]
    a["w_pool"] = np.ascontiguousarray(pw.reshape(4, 2, P, 2, P).transpose(2, 0, 1, 3, 4)).reshape(1, P, 16 * P)
    for l, up, down in ((0, f("ffn_w_up")[0], f("ffn_w_down")[0]), (1, f("ffn_w_up")[1], f("ffn_w_down")[1]),
                        (2, f("w_gate_upffn_2")[0], f("w_down_2")[0])):
        a[f"w_up{l}"] = np.ascontiguousarray(up.reshape(DC, P, 2, FC, P).transpose(3, 1, 0, 2, 4)).reshape(FC, P, 16 * P)
        a[f"w_down{l}"] = _tiles(down, 1)
    gin = f("w_in_2")[0]
    o = np.cumsum([0, 256, 256, 512, 512, 16, 512, 512, 512])
    a["w_gin_a"] = _tiles(gin[:, np.r_[np.tile(np.arange(o[4], o[5]), 8), o[0]:o[1]]], 3)
    a["w_gin_k"] = _tiles(gin[:, o[1]:o[2]], 2)
    a["w_gin_v"] = _tiles(gin[:, o[2]:o[3]], 2)
    a["w_gin_g"] = _tiles(gin[:, o[3]:o[4]], 2)
    conv = [np.r_[o[6] + j * P:o[6] + (j + 1) * P, o[7] + j * P:o[7] + (j + 1) * P, o[5] + j * P:o[5] + (j + 1) * P]
            for j in range(4)]
    a["w_gin_c"] = _tiles(gin[:, np.concatenate(conv)], 3)
    a["w_wout"] = _tiles(f("w_out_2")[0], 2)
    a["w_pproj"] = _tiles(f("w_ple_proj_2")[0], 8)
    a["w_pgate"] = _tiles(f("w_ple_gate_2")[0], 2)
    par = {}
    for l in range(2):
        par[f"mix_pre{l}"], par[f"mix_post{l}"] = f("norm_mix_pre")[l], f("norm_mix_post")[l]
        par[f"ffn_pre{l}"], par[f"ffn_post{l}"] = f("norm_ffn_pre")[l], f("norm_ffn_post")[l]
        par[f"cw{l}"], par[f"cb{l}"] = f("ffn_conv_w")[l], f("ffn_conv_b")[l]
    par.update(q_norm=f("mla_q_norm")[0], kv_norm=f("mla_kv_norm")[0], pool_scale=f("pool_scale")[0],
               ln1=f("ln1_g_2")[0], ln2=f("ln2_g_2")[0], ln3=f("ln3_g_2")[0], lnf=f("lnf_g_2"),
               b_gate=f("b_gate_2")[0], conv2=f("conv_w_2")[0], gn=f("gn_g_2")[0])
    a["par"] = np.ascontiguousarray(np.concatenate([_columns(par[name]) for name in PCOLS], axis=1))
    a["ident"] = np.eye(P, dtype=np.float32)
    inv = (1.0 / (np.float32(10000.0) ** (np.arange(0, ROPE, 2, dtype=np.float32) / ROPE))).astype(np.float32)
    ang = (np.arange(T1, dtype=np.float32)[:, None] * inv[None, :]).astype(np.float32)
    cos, sin = np.cos(ang).T, np.sin(ang).T
    a["rope"] = np.ascontiguousarray(np.stack([np.tile(cos, (8, 1)), np.tile(np.concatenate([-sin, sin]), (4, 1))], axis=1)
                                     .astype(np.float32))
    q, k = np.indices((96, 96))
    a["cmask"] = np.where(q >= k, 0.0, -1e30).astype(np.float32)
    count = np.stack([1.0 / np.minimum(np.arange(1, T1 + 1), w) for w in WINDOWS]).astype(np.float32)
    a["icnt"] = np.ascontiguousarray(np.broadcast_to(count, (P, 4, T1)))
    s, t = np.indices((P, P))
    masks = [(s >> (l + 1) == t >> (l + 1)) & ((s >> l) % 2 == 0) & ((t >> l) % 2 == 1) for l in range(7)] + [s == t]
    a["lmask"] = np.ascontiguousarray(np.stack(masks, axis=1).astype(np.int32))
    return a


def kernel(**inputs):
    import concourse.bacc as bacc
    from concourse.bass_utils import run_bass_kernel_spmd

    arrays = _layout(inputs)
    marks = {}
    for final in (False, True):
        nc = bacc.Bacc("TRN2", target_bir_lowering=False, num_devices=1)
        dram = {name: nc.dram_tensor(f"{name}_dram", a.shape, mybir.dt.from_np(a.dtype), kind="ExternalInput").ap()
                for name, a in arrays.items()}
        dram["out"] = nc.dram_tensor("out_dram", (P, DC, SEQ), F32, kind="ExternalOutput").ap()
        program(nc, dram, marks, final)
    r = run_bass_kernel_spmd(nc, [{f"{name}_dram": a for name, a in arrays.items()}], core_ids=[0])
    out = np.asarray(r.results[0]["out_dram"])
    return np.ascontiguousarray(out.transpose(2, 1, 0).reshape(1, SEQ, D))
```

```python
from contextlib import ExitStack

import numpy as np

import concourse.bass as bass
from concourse import mybir

F32 = mybir.dt.float32
F32R = mybir.dt.float32r
I32 = mybir.dt.int32
ALU = mybir.AluOpType
ACT = mybir.ActivationFunctionType
AX = mybir.AxisListType.X

LOOPED = ("e", "fpost0", "fpost1")
P = 128
D = 1024
DC = D // P
META, SEQ = 16, 256
T1 = META + SEQ
FF = 2816
FC = FF // P
NH, NOPE, ROPE, VD = 16, 64, 32, 64
QR, KVR = 384, 256
QC, KC = QR // P, KVR // P
TQ = 96
QT = [(0, 96), (96, 96), (192, 80)]
TT = [(0, P), (P, P), (2 * P, T1 - 2 * P)]
WIN_AT = [0, T1, T1 + (T1 - P)]
WIN = T1 + (T1 - P) + (T1 - 2 * P)
PTOFF = [0, T1, T1 + 176]
SCALE = float(NOPE + ROPE) ** -0.5
EPS = 1e-6
WINDOWS = (2, 4, 8, 16)
GH, GDK, GDV = 4, 64, 128
FAR, DIAGONAL = 7, 8
LEVEL_ORDER = [DIAGONAL] + list(range(8))
FIRST_LEVEL = LEVEL_ORDER[0]
LEVEL_BEFORE = {b: a for a, b in zip(LEVEL_ORDER, LEVEL_ORDER[1:])}
SLOT = 24 * P
NORM_BANK, R_BANK = 6, 7
GUESS, GUESS_A, GUESS_B = 0x5F1FFFF9, 0.703952253, 2.38924456

PIECES = DC // 2

PCOLS = {}


def _place(names):
    at = 0
    for name, n in names:
        PCOLS[name] = at
        at += n
    return at


NPAR = _place([("mix_pre0", 8), ("mix_pre1", 8), ("mix_post0", 8), ("mix_post1", 8),
               ("ffn_pre0", 8), ("ffn_pre1", 8), ("ffn_post0", 8), ("ffn_post1", 8),
               ("q_norm", QC), ("kv_norm", KC), ("pool_scale", 8),
               ("cw0", 3 * 2 * FC), ("cw1", 3 * 2 * FC), ("cb0", 2 * FC), ("cb1", 2 * FC),
               ("ln1", 8), ("ln2", 8), ("ln3", 8), ("lnf", 8),
               ("b_gate", 2), ("conv2", 12), ("gn", 1)])

STREAM = [
    ("dq", 1, 24, 3, "v"), ("dkv", 1, 16, 2, "v"), ("dkr", 1, 16, 2, "v"),
    ("uqn", 1, 24, 8, "a"), ("uqr", 1, 24, 8, "v"), ("uk", 1, 16, 8, "a"), ("uv", 1, 16, 6, "v"),
    ("wo", 4, 16, 2, "a"),
    ("up0", FC, 16, 2, "v"), ("down0", DC, 22, 1, "a"),
    ("pool", 1, 16, 2 * len(TT) + 8, "a"),
    ("up1", FC, 16, 2, "v"), ("down1", DC, 22, 1, "a"),
    ("gin_a", 1, 24, 3, "v"), ("gin_k", 1, 16, 2, "v"), ("gin_v", 2, 16, 2, "a"),
    ("gin_g", 2, 16, 2, "v"), ("gin_c", 4, 24, 3, "v"),
    ("wout", 4, 16, 2, "v"),
    ("pproj", 1, 16, 8, "a"),
    ("up2", FC, 16, 2, "v"), ("down2", DC, 22, 1, "v"),
    ("pgate", 4, 16, 2, "v"),
]
FIRST_UNIT, FIRST_BLOCK, UNITS, BLOCKS = {}, {}, [], []
for _name, _units, _tiles, _blocks, _eng in STREAM:
    FIRST_UNIT[_name], FIRST_BLOCK[_name] = len(UNITS), len(BLOCKS)
    for _u in range(_units):
        _n = len(UNITS)
        for _b in range(_blocks):
            BLOCKS.append(dict(unit=_n, eng=_eng, bank=(3 * (_n % 2) + _b) % 6,
                               freed=1 + sum(1 for x in BLOCKS if x["eng"] == _eng)))
        UNITS.append(dict(name=_name, u=_u, tiles=_tiles, first=len(BLOCKS) - _blocks, blocks=_blocks))
BY_NAME = {s[0]: s for s in STREAM}
for _i, _x in enumerate(BLOCKS):
    _x["before"] = next((j for j in range(_i - 1, -1, -1) if BLOCKS[j]["bank"] == _x["bank"]), None)


def vector_cols(n):
    return UNITS[n]["tiles"] * P // 3 if UNITS[n]["name"] == "uqn" else (3 * UNITS[n]["tiles"] // 4) * P


class Steps:

    def __init__(self, engine, sem, marks):
        self.engine, self.sem, self.marks = engine, sem, marks
        self.n, self.i = 0, None

    def enter(self, label, i):
        self.label, self.i, self.base = label, i, self.n
        self.stride = self.marks.get(("stride", self.engine, label), 1)

    def leave(self, iterations):
        stride = self.n - self.base
        self.marks[("stride", self.engine, self.label)] = stride
        self.n, self.i = self.base + stride * iterations, None

    def step(self, name=None):
        self.n += 1
        if name is not None:
            self.marks[name] = (self.engine, self.n, self.label if self.i is not None else None)
        return self.sem, 1

    def now(self):
        return self.sem, self.n if self.i is None else self.i * self.stride + self.n


def program(nc, dram, marks, final):
    ctx = ExitStack()
    with ctx:
        def sb(name, shape, dt=F32, stack=None):
            return (stack or ctx).enter_context(nc.sbuf_tensor(name, shape, dt))

        def sem(name):
            return ctx.enter_context(nc.semaphore(name))

        step_sems = {e: sem(f"{e}_steps") for e in ("vector", "scalar", "pool", "tensor")}

        def done(name, i=None):
            engine, n, loop = marks.get(name, ("scalar", 1, None))
            stride = marks.get(("stride", engine, loop), 1)
            if final and name not in marks:
                raise KeyError(name)
            if isinstance(i, tuple):
                i, n = i[0], n - i[1] * stride
            return step_sems[engine], n if i is None else i * stride + n

        products = sem("products")
        high_parts, low_parts_v, low_parts_g = sem("high_parts"), sem("low_parts_v"), sem("low_parts_g")
        freed = {"v": sem("freed_v"), "a": sem("freed_a")}
        loaded = [sem("weights_loaded_0"), sem("weights_loaded_1")]
        tables_in = sem("tables_in")
        h_in = [sem(f"h_in_{c}") for c in range(PIECES)]
        pieces_in = [sem(f"first_unit_in_{c}") for c in range(PIECES - 1)]
        gains_in = sem("first_gains_in")
        p_in = sem("p_in")
        out_written = sem("out_written")

        raw = [sb(f"raw{s}", [P, SLOT]) for s in range(2)]
        wh = [sb(f"w_high{s}", [P, SLOT], F32R) for s in range(2)]
        wl = [sb(f"w_low{s}", [P, SLOT], F32R) for s in range(2)]
        par = sb("par", [P, NPAR])
        ident = sb("ident", [P, P])
        ones = sb("ones", [P, P])
        h = sb("h", [P, DC, T1])
        m = sb("m", [P, DC, T1])
        uh = sb("u_high", [P, DC, T1], F32R)
        ul = sb("u_low", [P, DC, T1], F32R)
        acc = sb("acc", [P, 2, 3 * P])
        sq = sb("sq", [P, 2, 3 * P])
        rows = sb("r_rows", [P, T1])
        nx = sb("norm_x", [P, 8])
        nh = sb("norm_half", [P, 8])
        nt = sb("norm_t", [P, 8])
        ny = sb("norm_y", [P, 8])
        nr = sb("norm_1_by_rms", [P, 8])
        warm = sb("warm", [P, 1])
        psg = sb("pool_gains", [P, 8])
        diag = sb("norm_diag", [P, 8 * P])
        ur = sb("conv_in", [P, 2, 2 + T1])
        cv = sb("conv_out", [P, 2, T1])
        xf = sb("x_full", [P, T1])

        mla = ExitStack()
        Q = sb("q_heads", [96, NH, T1], stack=mla)
        K = sb("k_heads", [96, NH, T1], stack=mla)
        V = sb("v_tokens", [96, 3, D], stack=mla)
        mla.close()
        xh = sb("x_high", [P, FC, T1], F32R)
        xl = sb("x_low", [P, FC, T1], F32R)
        att = ExitStack()
        rope = sb("rope", [P, 2, T1], stack=att)
        ropeR = sb("rope_r", [P, 2, T1], stack=att)
        ra = sb("rope_a", [P, T1], stack=att)
        rb = sb("rope_b", [P, T1], stack=att)
        kr = sb("k_rope", [P, T1], stack=att)
        cmask = sb("causal", [96, 96], stack=att)
        mx = sb("row_max", [96, 2, 3], stack=att)
        nb = sb("neg_max", [96, 2, 3], stack=att)
        sm = sb("row_sum", [96, 2, 3], stack=att)
        rc = sb("row_inv", [96, 2, 3], stack=att)
        Pp = sb("probs", [96, 2, 560], stack=att)
        PT = sb("probs_t", [96, 2, 528], stack=att)
        att.close()
        pl = ExitStack()
        pz = sb("pool_z", [P, 3, D], stack=pl)
        wm = sb("window_means", [P, 4, WIN], stack=pl)
        pl.close()
        gq = sb("gla_q", [P, 512])
        gk = sb("gla_k", [P, 512])
        pre = sb("gla_pre", [P, 512])
        suf = sb("gla_suf", [P, 512])
        eq = sb("gla_exp_pre", [P, 512])
        ek = sb("gla_exp_suf", [P, 512])
        ql = sb("gla_q_level", [P, 512])
        kl = sb("gla_k_level", [P, 512])
        gv = sb("gla_v", [P, 2, 512])
        Sd = sb("gla_s_diag", [P, 2, 4 * P])
        S01 = sb("gla_s_far", [P, 2, 2 * P])
        lmask = sb("level_masks", [P, 8, P], I32)
        wgu = sb("w_gate_up", [16, 256])
        glr = sb("gate_low_rank", [P, 256])

        bank = [ctx.enter_context(nc.psum_tensor(f"bank{b}", [P, 512], F32)) for b in range(8)]

        def pcol(name, j=0, n=1):
            return par[:, bass.ds(PCOLS[name] + j, n)]

        block = ctx.enter_context(nc.Block())

        def through(n):
            return UNITS[n]["first"] + UNITS[n]["blocks"]

        def first_pieces():
            w = UNITS[0]["tiles"] * P // PIECES
            return [slice(p * w, (p + 1) * w) for p in range(PIECES)]

        @block.sync
        def _(sp):
            sp.dma_start(par[:, 0:DC], dram["par"][:, 0:DC]).then_inc(gains_in, 16)
            for p, cols in enumerate(first_pieces()):
                sp.dma_start(h[:, 2 * p:2 * p + 2, :], dram["h0"][:, 2 * p:2 * p + 2, :]).then_inc(h_in[p], 16)
                sp.dma_start(raw[0][:, cols], dram["w_dq"][0, :, cols])\
                    .then_inc(loaded[0] if p == PIECES - 1 else pieces_in[p], 16)

            def slot_free(n):
                sp.wait_ge(high_parts, n - 1)
                sp.wait_ge(low_parts_v, n - 1)
                sp.wait_ge(low_parts_g, n - 1)

            for name, units, tiles, _, _ in STREAM:
                n0, cols, src = FIRST_UNIT[name], tiles * P, dram["w_" + name]
                if units < 8:
                    for u in range(units):
                        n = n0 + u
                        if n == 0:
                            continue
                        if n >= 2:
                            slot_free(n)
                        sp.dma_start(raw[n % 2][:, 0:cols], src[u, :, :]).then_inc(loaded[n % 2], 16)
                        if n == 1:
                            for dst, src_ in ((ident[:, :], dram["ident"]), (par[:, DC:NPAR], dram["par"][:, DC:NPAR]),
                                              (rope[:, :, :], dram["rope"]), (cmask[:, :], dram["cmask"])):
                                sp.dma_start(dst, src_).then_inc(tables_in, 16)
                else:
                    with sp.Fori(0, units // 2) as i:
                        for k in range(2):
                            n = 2 * i + (n0 + k)
                            slot_free(n)
                            sp.dma_start(raw[(n0 + k) % 2][:, 0:cols], src[2 * i + k, :, :])\
                                .then_inc(loaded[(n0 + k) % 2], 16)
                if name == "down0":
                    sp.wait_ge(*done("att out 7 low"))
                    sp.dma_start(wm[:, :, :], dram["window_means"]).then_inc(tables_in, 16)
                if name == "down1":
                    sp.wait_ge(products, through(FIRST_UNIT["pool"]))
                    sp.dma_start(lmask[:, :, :], dram["lmask"]).then_inc(tables_in, 16)
                    sp.dma_start(wgu[:, :], dram["wgu"]).then_inc(tables_in, 16)
                if name == "wout":
                    sp.wait_ge(*done("conv y low 3"))
                    sp.dma_start(cv[:, :, 0:SEQ], dram["p_t"]).then_inc(p_in, 16)
            for c in range(2):
                sp.wait_ge(*done(f"final {4 * c + 3}"))
                sp.dma_start(dram["out"][:, 4 * c:4 * c + 4, :], m[:, 4 * c:4 * c + 4, 0:SEQ])\
                    .then_inc(out_written, 16)
            sp.wait_ge(out_written, 32)

        def first_half(n):
            return vector_cols(n) // P // 2 * P

        def up_place(j):
            return (j, None) if j < 2 or j >= FC - 2 else (f"k{j % 2}", (j - 2) // 2)

        def up_turns(eng, S, l, turn):
            for j in range(2):
                turn(j, up_place(j), up_place(j - 1) if j else None)
            with eng.Fori(0, (FC - 4) // 2) as i:
                S.enter(f"up{l}", i)
                for k in range(2):
                    turn(2 * i + (2 + k), (f"k{k}", i), ("k0", i) if k else ("k1", (i, 1)))
                S.leave((FC - 4) // 2)
            for j in range(FC - 2, FC):
                turn(j, up_place(j), up_place(j - 1))

        @block.tensor
        def _(pe):
            S = Steps("tensor", step_sems["tensor"], marks)

            def parts_ready(n, i=None):
                at = n + 1 if i is None else 2 * i + (n + 1)
                pe.wait_ge(high_parts, at)
                pe.wait_ge(low_parts_v, at)
                pe.wait_ge(low_parts_g, at)

            def bank_free(b, i=None, stride=0):
                before = BLOCKS[b]["before"]
                if before is not None:
                    x = BLOCKS[before]
                    pe.wait_ge(freed[x["eng"]], x["freed"] if i is None else i * stride + x["freed"])

            def three(out, hi, lo, rhi, rlo, start, stop):
                nc.tensor.matmul(out, hi, rhi, start=start, stop=False)
                nc.tensor.matmul(out, hi, rlo, start=False, stop=False)
                return nc.tensor.matmul(out, lo, rhi, start=False, stop=stop)

            def weights(n, j):
                return wh[n % 2][:, j * P:(j + 1) * P], wl[n % 2][:, j * P:(j + 1) * P]

            def unit(n, T, xs, chunk_ready=None, middle=None, i=None, order=None):
                U = UNITS[n]
                nb, kc = U["blocks"], U["tiles"] // U["blocks"]
                if n > 0:
                    parts_ready(n, i)
                for b in range(nb):
                    bank_free(U["first"] + b, i, 2 * nb)
                for at, k in enumerate(order or range(kc)):
                    if chunk_ready is not None:
                        chunk_ready(k)
                    if middle is not None and at == kc // 2:
                        middle()
                    for b in range(nb):
                        hi, lo = weights(n, k * nb + b)
                        last = three(bank[BLOCKS[U["first"] + b]["bank"]][:, 0:T], hi, lo,
                                     xs[0][:, k, 0:T], xs[1][:, k, 0:T], at == 0, at == kc - 1)
                        if at == kc - 1:
                            last.then_inc(products, 1)

            def blocks_in_turn(n, T, operands, kc):
                U = UNITS[n]
                parts_ready(n)
                for b in range(U["blocks"]):
                    bank_free(U["first"] + b)
                    for k in range(kc):
                        hi, lo = weights(n, k * U["blocks"] + b)
                        rhi, rlo = operands(b, k)
                        last = three(bank[BLOCKS[U["first"] + b]["bank"]][:, 0:T], hi, lo, rhi, rlo,
                                     k == 0, k == kc - 1)
                    last.then_inc(products, 1)

            def norm_sums(name, after, squares, last_chunk=False):
                pe.wait_ge(*done(after))
                if last_chunk:
                    pe.wait_ge(*done(f"{name} sq {DC - 1}"))
                for c, x in enumerate(squares):
                    out = bank[NORM_BANK][:, c:c + 1]
                    last = nc.tensor.matmul(out, x, ones[:, 0:1], start=True, stop=not last_chunk)
                    if last_chunk:
                        x = sq[:, (DC - 1) % 2, c * P:(c + 1) * P]
                        last = nc.tensor.matmul(out, x, ones[:, 0:1], start=False, stop=True)
                last.then_inc(*S.step(f"{name} sums"))

            def norm_rows(name, outs):
                pe.wait_ge(*done(f"{name} diagonal"))
                for c, out in enumerate(outs):
                    last = nc.tensor.matmul(out, ones[:, :], diag[:, c * P:c * P + out.shape[1]], start=True, stop=True)
                last.then_inc(*S.step(f"{name} rows"))

            def token_rows(b, n, at=0):
                return [bank[b][:, at + i * P:at + min((i + 1) * P, n)] for i in range(-(-n // P))]

            def u_ready(name):
                def wait(c):
                    i, k = (c // 2, c % 2) if name == "e" and c < DC - 2 else (None, c)
                    pe.wait_ge(*done(f"{name} u high {k}", i))
                    pe.wait_ge(*done(f"{name} u low {k}", i))
                return wait

            def squares(a, n):
                return [acc[:, a, i * P:(i + 1) * P] for i in range(-(-n // P))]

            def ffn_up(l, T, sums_name):
                n0 = FIRST_UNIT[f"up{l}"]
                us = (uh, ul)
                unit(n0, T, us, u_ready(sums_name))
                norm_sums(sums_name, f"{sums_name} acc {DC - 2}", squares(0, T), True)
                unit(n0 + 1, T, us, None, lambda: norm_rows(sums_name, token_rows(R_BANK, T)))
                with pe.Fori(0, (FC - 2) // 2) as i:
                    for k in range(2):
                        unit(n0 + 2 + k, T, us, i=i)

            def ffn_down(l, T):
                n0 = FIRST_UNIT[f"down{l}"]

                def x_ready(j):
                    k, i = up_place(j + 1 if l < 2 else j)
                    pe.wait_ge(*done(f"x high {l} {k}", i))
                    pe.wait_ge(*done(f"x low {l} {k}", i))
                unit(n0, T, (xh, xl), x_ready)
                unit(n0 + 1, T, (xh, xl))
                with pe.Fori(0, (DC - 2) // 2) as i:
                    for k in range(2):
                        unit(n0 + 2 + k, T, (xh, xl), i=i)

            pe.wait_ge(*done("constants"))
            n = FIRST_UNIT["dq"]

            def piece_ready(k):
                p = k // 2
                if p == PIECES - 1:
                    parts_ready(0)
                else:
                    pe.wait_ge(*done(f"first high {p}"))
                    pe.wait_ge(*((low_parts_v, 1) if p == PIECES - 2 else done(f"first low {p}")))
                u_ready("a0")(k)
            unit(n, T1, (uh, ul), piece_ready)
            norm_sums("a0", f"a0 acc {DC - 2}", squares(0, T1), True)
            unit(n + 1, T1, (uh, ul), None, lambda: norm_rows("a0", token_rows(R_BANK, T1)))
            unit(n + 2, T1, (uh, ul), None,
                 lambda: norm_sums("c", "kv squares", squares(0, T1) + squares(1, T1)))
            norm_rows("c", token_rows(R_BANK, T1) + token_rows(NORM_BANK, T1, P))
            for k in range(QC):
                u_ready("c")(k)
            for name in ("uqn", "uqr"):
                blocks_in_turn(FIRST_UNIT[name], T1, lambda b, k: (uh[:, k, :], ul[:, k, :]), QC)
            for k in range(QC, QC + KC):
                u_ready("c")(k)
            blocks_in_turn(FIRST_UNIT["uk"], T1, lambda b, k: (uh[:, QC + k, :], ul[:, QC + k, :]), KC)
            n = FIRST_UNIT["uv"]
            parts_ready(n)
            for half in range(2):
                for t, (q0, nq) in enumerate(QT):
                    b = UNITS[n]["first"] + half * 3 + t
                    bank_free(b)
                    out = bank[BLOCKS[b]["bank"]][0:nq, :]
                    for k in range(KC):
                        at = slice(k * D + half * 512, k * D + half * 512 + 512)
                        toks = slice(q0, q0 + nq)
                        nc.tensor.matmul(out, uh[:, QC + k, toks], wh[n % 2][:, at], start=k == 0, stop=False)
                        nc.tensor.matmul(out, uh[:, QC + k, toks], wl[n % 2][:, at], start=False, stop=False)
                        last = nc.tensor.matmul(out, ul[:, QC + k, toks], wh[n % 2][:, at],
                                                start=False, stop=k == KC - 1)
                    last.then_inc(products, 1)

            pe.wait_ge(*done("k rope"))
            pe.wait_ge(freed["v"], BLOCKS[FIRST_BLOCK["uv"] + 5]["freed"])
            pe.wait_ge(tables_in, 64)
            for s in range(-1, NH + 2):
                if s + 1 < NH:
                    g = s + 1
                    X, Y = bank[g % 2], bank[2 + g % 2]
                    if g >= 2:
                        pe.wait_ge(*done(f"exp {g - 2}"))
                    for out, (q0, nq) in ((X[0:96, 0:96], QT[0]), (X[0:96, 96:288], QT[1]), (Y[0:80, 0:T1], QT[2])):
                        last = nc.tensor.matmul(out, Q[:, g, q0:q0 + nq], K[:, g, 0:q0 + nq], start=True, stop=True)
                    last.then_inc(*S.step(f"scores {g}"))
                if s >= 2:
                    g = s - 2
                    pair, half = g // 2, g % 2
                    pe.wait_ge(*done(f"transposed a {g}"))
                    pe.wait_ge(*done(f"transposed b {g}"))
                    if half == 0 and pair >= 2:
                        pe.wait_ge(*done(f"att out {pair - 2} low"))
                    o = bank[6 + pair % 2][64 * half:64 * half + 64, :]
                    for c, (k0, nk) in enumerate(QT):
                        last = nc.tensor.matmul(o[:, k0:T1], V[0:nk, c, g * VD:(g + 1) * VD],
                                                PT[0:nk, g % 2, PTOFF[c]:PTOFF[c] + T1 - k0],
                                                start=c == 0, stop=c == 2)
                    last.then_inc(*S.step(f"values {g}"))
                if 1 <= s <= NH:
                    g = s - 1
                    pe.wait_ge(*done(f"probs {g}"))
                    if g >= 1:
                        pe.wait_ge(*done(f"transposed a {g - 1}"))
                        pe.wait_ge(*done(f"transposed b {g - 1}"))
                    at = (0, 96, 288)
                    for out, t, c in ((bank[4][0:96, 0:96], 0, 0), (bank[4][0:96, 96:192], 1, 0),
                                      (bank[4][0:96, 192:272], 2, 0), (bank[5][0:96, 0:96], 1, 1),
                                      (bank[5][0:96, 96:176], 2, 1), (bank[5][0:80, 176:256], 2, 2)):
                        nq, nk = QT[t][1], QT[c][1]
                        src = Pp[0:nq, g % 2, at[t] + 96 * c:at[t] + 96 * c + nk]
                        last = nc.tensor.transpose(out, src, ident[0:nq, 0:nq])
                    last.then_inc(*S.step(f"transposes {g}"))

            n = FIRST_UNIT["wo"]

            def att_ready(k):
                pe.wait_ge(*done(f"att out {k} high"))
                pe.wait_ge(*done(f"att out {k} low"))
            for u in range(4):
                unit(n + u, T1, (uh, ul), att_ready if u == 0 else None)
            norm_sums("post0", f"post0 acc {DC - 2}", squares(0, T1), True)
            norm_rows("post0", token_rows(R_BANK, T1))
            ffn_up(0, T1, "f0")
            ffn_down(0, T1)
            norm_sums("fpost0", f"fpost0 acc {DC - 2}", squares(0, T1), True)
            norm_rows("fpost0", token_rows(R_BANK, T1))

            n = FIRST_UNIT["pool"]
            first = UNITS[n]["first"]
            parts_ready(n)
            for half in range(2):
                for t, (t0, nt_) in enumerate(TT):
                    b = first + half * len(TT) + t
                    bank_free(b)
                    for g in range(2 * half, 2 * half + 2):
                        out = bank[BLOCKS[b]["bank"]][0:nt_, (g % 2) * 256:(g % 2) * 256 + 256]
                        for k in range(2):
                            if t == 0:
                                u_ready("a1")(2 * g + k)
                            toks, at = slice(t0, t0 + nt_), slice((g * 2 + k) * 256, (g * 2 + k) * 256 + 256)
                            nc.tensor.matmul(out, uh[:, 2 * g + k, toks], wh[n % 2][:, at], start=k == 0, stop=False)
                            nc.tensor.matmul(out, uh[:, 2 * g + k, toks], wl[n % 2][:, at], start=False, stop=False)
                            last = nc.tensor.matmul(out, ul[:, 2 * g + k, toks], wh[n % 2][:, at],
                                                    start=False, stop=k == 1)
                    last.then_inc(products, 1)
                if half == 0:
                    norm_sums("a1", f"a1 acc {DC - 2}", squares(0, T1), True)
            pe.wait_ge(tables_in, 80)
            for c in range(DC):
                half, g = c // 4, c // 2
                pe.wait_ge(freed["a"], BLOCKS[first + half * len(TT) + len(TT) - 1]["freed"])
                b = first + 2 * len(TT) + c
                bank_free(b)
                for t, (t0, nt_) in enumerate(TT):
                    last = nc.tensor.matmul(bank[BLOCKS[b]["bank"]][:, t0:T1], pz[0:nt_, t, c * P:(c + 1) * P],
                                            wm[0:nt_, g, WIN_AT[t]:WIN_AT[t] + T1 - t0],
                                            start=t == 0, stop=t == len(TT) - 1)
                last.then_inc(products, 1)
            norm_sums("post1", f"post1 acc {DC - 2}", squares(0, T1), True)
            norm_rows("post1", token_rows(R_BANK, T1))
            ffn_up(1, T1, "f1")
            ffn_down(1, T1)
            norm_sums("fpost1", f"fpost1 acc {DC - 2}", squares(0, T1), True)
            norm_rows("fpost1", token_rows(R_BANK, T1))

            def level(l):
                if l == DIAGONAL:
                    pe.wait_ge(freed["v"], BLOCKS[FIRST_BLOCK["gin_k"] + 1]["freed"])
                    pe.wait_ge(*done("gate inputs"))
                else:
                    pe.wait_ge(*done(f"level {l} q"))
                    pe.wait_ge(*done(f"level {l} k"))
                    pe.wait_ge(*done(f"level {LEVEL_BEFORE[l]} kept 1"))
                qs, ks = (gq, gk) if l == DIAGONAL else (ql, kl)
                for half in range(2):
                    part = slice(64 * half, 64 * half + 64)
                    for pair in range(2):
                        for i in range(2):
                            if l == FAR and i:
                                continue
                            j = 1 if l == FAR else i
                            o = (pair if l == FAR else pair * 2 + i) * P
                            last = nc.tensor.matmul(bank[6 + half][:, o:o + P],
                                                    ks[part, pair * SEQ + i * P:pair * SEQ + (i + 1) * P],
                                                    qs[part, pair * SEQ + j * P:pair * SEQ + (j + 1) * P],
                                                    start=True, stop=True)
                last.then_inc(*S.step(f"level {l} scores"))

            n = FIRST_UNIT["gin_a"]
            T = SEQ
            us = (uh, ul)
            unit(n, T, us, u_ready("g"))
            norm_sums("g", f"g acc {DC - 2}", squares(0, T), True)
            unit(n + 1, T, us, None, lambda: norm_rows("g", token_rows(R_BANK, T)))
            pe.wait_ge(freed["v"], BLOCKS[FIRST_BLOCK["gin_a"]]["freed"])
            pe.wait_ge(tables_in, 16 * 7)
            for pair in range(2):
                last = nc.tensor.matmul(bank[6][:, pair * SEQ:(pair + 1) * SEQ], wgu[:, pair * P:(pair + 1) * P],
                                        glr[0:16, :], start=True, stop=True)
            last.then_inc(*S.step("gate logits"))
            for v in range(2):
                n = FIRST_UNIT["gin_v"] + v
                parts_ready(n)
                for t in range(2):
                    b = UNITS[n]["first"] + t
                    bank_free(b)
                    out = bank[BLOCKS[b]["bank"]][:, 0:256]
                    for k in range(DC):
                        toks, at = slice(t * P, (t + 1) * P), slice(k * 256, (k + 1) * 256)
                        nc.tensor.matmul(out, uh[:, k, toks], wh[n % 2][:, at], start=k == 0, stop=False)
                        nc.tensor.matmul(out, uh[:, k, toks], wl[n % 2][:, at], start=False, stop=False)
                        last = nc.tensor.matmul(out, ul[:, k, toks], wh[n % 2][:, at], start=False, stop=k == DC - 1)
                    last.then_inc(products, 1)
            def gla_out():
                pe.wait_ge(*done(f"level {LEVEL_ORDER[8]} kept 1"))
                pe.wait_ge(freed["a"], BLOCKS[FIRST_BLOCK["gin_v"] + 3]["freed"])
                for head in range(GH):
                    pair, half = head // 2, head % 2
                    o = bank[6 + pair]
                    at, ch = half * SEQ, slice(head * P, (head + 1) * P)
                    nc.tensor.matmul(o[:, at:at + P], gv[:, 0, ch], Sd[:, half, pair * 2 * P:(pair * 2 + 1) * P],
                                     start=True, stop=True)
                    nc.tensor.matmul(o[:, at + P:at + 2 * P], gv[:, 0, ch], S01[:, half, pair * P:(pair + 1) * P],
                                     start=True, stop=False)
                    last = nc.tensor.matmul(o[:, at + P:at + 2 * P], gv[:, 1, ch],
                                            Sd[:, half, (pair * 2 + 1) * P:(pair * 2 + 2) * P], start=False, stop=True)
                last.then_inc(*S.step("gla out"))

            def gla_norm_sums():
                norm_sums("gn", "gla out squares",
                          [(eq, ek)[c // 4][:, (c % 4) * P:(c % 4 + 1) * P] for c in range(8)])

            def gla_norm_rows():
                norm_rows("gn", [bank[6 + c // 4][:, (c % 4) * P:(c % 4 + 1) * P] for c in range(8)])

            level(LEVEL_ORDER[0])
            unit(FIRST_UNIT["gin_g"], T, us)
            level(LEVEL_ORDER[1])
            unit(FIRST_UNIT["gin_g"] + 1, T, us, None, lambda: level(LEVEL_ORDER[2]))
            level(LEVEL_ORDER[3])
            unit(FIRST_UNIT["gin_c"], T, us, None, lambda: level(LEVEL_ORDER[4]))
            level(LEVEL_ORDER[5])
            unit(FIRST_UNIT["gin_c"] + 1, T, us, None, lambda: level(LEVEL_ORDER[6]))
            level(LEVEL_ORDER[7])
            unit(FIRST_UNIT["gin_c"] + 2, T, us, None, lambda: level(LEVEL_ORDER[8]))
            gla_out()
            unit(FIRST_UNIT["gin_c"] + 3, T, us, None, gla_norm_sums)
            gla_norm_rows()

            def mix_ready(k):
                kind = "gla mix" if k < 4 else "conv y"
                pe.wait_ge(*done(f"{kind} high {k % 4}"))
                pe.wait_ge(*done(f"{kind} low {k % 4}"))
            for u in range(4):
                unit(FIRST_UNIT["wout"] + u, T, (xh, xl), mix_ready if u == 0 else None,
                     order=(4, 5, 6, 0, 1, 2, 3, 7) if u == 0 else None)
            for k in range(2):
                pe.wait_ge(*done(f"p high {k}"))
                pe.wait_ge(*done(f"p low {k}"))
            blocks_in_turn(FIRST_UNIT["pproj"], T, lambda b, k: (xh[:, 8 + k, 0:T], xl[:, 8 + k, 0:T]), 2)
            ffn_up(2, T, "f2")
            ffn_down(2, T)
            n = FIRST_UNIT["pgate"]
            unit(n, T, us, u_ready("e"))
            norm_sums("e", f"e acc {DC - 2}", squares(0, T), True)
            unit(n + 1, T, us, None, lambda: norm_rows("e", token_rows(R_BANK, T)))
            unit(n + 2, T, us)
            unit(n + 3, T, us)
            norm_sums("out", f"out acc {DC - 2}", squares(0, T), True)
            norm_rows("out", token_rows(R_BANK, T))

        @block.scalar
        def _(act):
            S = Steps("scalar", step_sems["scalar"], marks)

            def high(n, i=None, first=None, middle=None):
                cols, U = UNITS[n]["tiles"] * P, UNITS[n]
                at = 16 * (n // 2 + 1)
                act.wait_ge(loaded[n % 2], at if i is None else 16 * i + at)
                if n >= 2:
                    at = through(n - 2)
                    act.wait_ge(products, at if i is None else i * 2 * UNITS[n - 2]["blocks"] + at)
                split = first_half(n) if first else 0
                if first:
                    nc.scalar.activation(wh[n % 2][:, 0:split], raw[n % 2][:, 0:split], ACT.Copy).then_inc(*S.step(first))
                if middle:
                    middle()
                nc.scalar.activation(wh[n % 2][:, split:cols], raw[n % 2][:, split:cols], ACT.Copy).then_inc(high_parts, 1)

            def block_done(b, i=None, stride=0):
                act.wait_ge(products, b + 1 if i is None else i * stride + (b + 1))

            def square(name, c, src, T, sem_and_1, k=None, i=None):
                if i is not None and name != "e":
                    act.wait_ge(*done(f"{name} acc {k}", (i, 1)))
                elif i is not None:
                    pass
                elif c >= 2 and name in LOOPED:
                    act.wait_ge(*done(f"{name} acc {c % 2}", (DC - 4) // 2))
                elif c >= 2:
                    act.wait_ge(*done(f"{name} acc {c - 2}"))
                nc.scalar.activation(sq[:, (c if k is None else k) % 2, 0:T], src, ACT.Square).then_inc(*sem_and_1)

            def u_high(name, c, T, t0, gain, k=None, i=None):
                label = c if k is None else k
                if i is not None:
                    act.wait_ge(*done(f"{name} acc {k}", (i, 1)))
                nc.scalar.activation(uh[:, c, 0:T], h[:, c, t0:t0 + T], ACT.Copy, scale=pcol(gain, c))\
                    .then_inc(*S.step(f"{name} u high {label}"))
                square(name, c, h[:, c, t0:t0 + T], T, S.step(f"{name} sq {label}"), k, i)

            def post(name, c, n, b, gain, k=None, i=None, stride=0, scale=None):
                src = bank[BLOCKS[b]["bank"]][:, 0:T1]
                if scale is not None:
                    if c >= 2:
                        act.wait_ge(*done(f"{name} acc {c - 2}"))
                    block_done(b, i, stride)
                    nc.scalar.activation(sq[:, c % 2, 0:T1], src, ACT.Square, scale=scale)\
                        .then_inc(*S.step(f"{name} sq {c}"))
                else:
                    block_done(b, i, stride)
                    square(name, c, src, T1, S.step(f"{name} sq {c if k is None else k}"), k, i)
                nc.scalar.activation(m[:, c, :], src, ACT.Copy,
                                     scale=gain if scale is not None else pcol(gain, c)).then_inc(freed["a"], 1)

            def ffn_up(l, T, conv):
                n0, b0 = FIRST_UNIT[f"up{l}"], FIRST_BLOCK[f"up{l}"]

                def x_high(turn_, j):
                    k, i = turn_
                    act.wait_ge(*done(f"x full {l} {k}", i))
                    nc.scalar.activation(xh[:, j, 0:T], xf[:, 0:T], ACT.Copy).then_inc(*S.step(f"x high {l} {k}"))

                def turn(j, place, before):
                    k, i = place
                    n = n0 + (j if i is None else 2 + int(k[1]))
                    U = UNITS[n]
                    high(n + 2, i, f"first high {l} {k}", middle=None if conv else lambda: silu(n, i, k))
                    if conv:
                        if before is not None:
                            act.wait_ge(*done(f"x full {l} {k}", i))
                        for hf in range(2):
                            B = BLOCKS[U["first"] + hf]
                            act.wait_ge(freed["v"], B["freed"] if i is None else 4 * i + B["freed"])
                            nc.scalar.activation(cv[:, hf, 0:T], ur[:, hf, 2:2 + T], ACT.Identity,
                                                 bias=pcol(f"cb{l}", hf * FC + j),
                                                 scale=pcol(f"cw{l}", (2 * 2 + hf) * FC + j))\
                                .then_inc(*S.step(f"tap 2 {l} {hf} {k}"))
                        if before is not None:
                            x_high(place, j - 1)
                        act.wait_ge(*done(f"taps {l} 0 {k}", i))
                        nc.scalar.activation(cv[:, 0, 0:T], cv[:, 0, 0:T], ACT.Silu).then_inc(*S.step(f"silu {l} {k}"))
                    else:
                        x_high(place, j)

                def silu(n, i, k):
                    B = BLOCKS[UNITS[n]["first"]]
                    act.wait_ge(freed["v"], B["freed"] if i is None else 4 * i + B["freed"])
                    nc.scalar.activation(cv[:, 0, 0:T], ur[:, 0, 2:2 + T], ACT.Silu).then_inc(*S.step(f"silu {l} {k}"))

                nc.scalar.activation(warm[:, :], ident[:, 0:1], ACT.Silu).then_inc(*S.step())
                up_turns(act, S, l, turn)
                if conv:
                    x_high(up_place(FC), FC - 1)

            def ffn_down(l):
                n0, b0 = FIRST_UNIT[f"down{l}"], FIRST_BLOCK[f"down{l}"]
                with act.Fori(0, (DC - 2) // 2) as i:
                    S.enter(f"down{l}", i)
                    for k in range(2):
                        post(f"fpost{l}", 2 * i + k, n0 + k, b0 + k, f"ffn_post{l}", k, i, 2)
                        high(n0 + k + 2, i)
                    S.leave((DC - 2) // 2)
                for c in range(DC - 2, DC):
                    post(f"fpost{l}", c, n0 + c, b0 + c, f"ffn_post{l}")
                    high(n0 + c + 2)

            act.wait_ge(*done("constants"))
            nc.scalar.activation(warm[:, :], ones[:, 0:1], ACT.Copy).then_inc(*S.step())
            act.wait_ge(gains_in, 16)
            for p, cols in enumerate(first_pieces()):
                if p < PIECES - 1:
                    act.wait_ge(pieces_in[p], 16)
                    signal = S.step(f"first high {p}")
                else:
                    act.wait_ge(loaded[0], 16)
                    signal = high_parts, 1
                nc.scalar.activation(wh[0][:, cols], raw[0][:, cols], ACT.Copy).then_inc(*signal)
                act.wait_ge(h_in[p], 16)
                for c in range(2 * p, 2 * p + 2):
                    u_high("a0", c, T1, 0, "mix_pre0")
            high(1)
            act.wait_ge(tables_in, 64)
            n = FIRST_UNIT["dq"]
            high(n + 2)
            for j in range(QC + KC):
                b = FIRST_BLOCK["dq"] + j
                act.wait_ge(freed["v"], BLOCKS[b]["freed"])
                if j >= 2:
                    act.wait_ge(*done(f"latent acc {j - 2}"))
                nc.scalar.activation(sq[:, j % 2, 0:T1], m[:, j, :], ACT.Square).then_inc(*S.step(f"latent sq {j}"))
            high(n + 3)
            for j in range(QC + KC):
                act.wait_ge(*done(f"latent {j}"))
                g = pcol("q_norm", j) if j < QC else pcol("kv_norm", j - QC)
                nc.scalar.activation(uh[:, j, :], m[:, j, :], ACT.Copy, scale=g).then_inc(*S.step(f"c u high {j}"))
            high(n + 4)
            act.wait_ge(*done("k rope full"))
            nc.scalar.activation(K[64:96, :, :], kr[64:96, :].unsqueeze(1).to_broadcast([32, NH, T1]), ACT.Copy)\
                .then_inc(*S.step("k rope"))

            def heads_out(name, dst):
                for b in range(8):
                    block_done(FIRST_BLOCK[name] + b)
                    src = bank[BLOCKS[FIRST_BLOCK[name] + b]["bank"]]
                    nc.scalar.activation(dst[0:64, 2 * b, :], src[0:64, 0:T1], ACT.Copy).then_inc(*S.step())
                    nc.scalar.activation(dst[0:64, 2 * b + 1, :], src[64:128, 0:T1], ACT.Copy)\
                        .then_inc(freed["a"], 1)
            heads_out("uqn", Q)
            high(FIRST_UNIT["uqn"] + 2)
            high(FIRST_UNIT["uqn"] + 3)
            heads_out("uk", K)
            high(FIRST_UNIT["uqn"] + 4)
            for s in range(NH + 4):
                if s == 2:
                    high(FIRST_UNIT["wo"] + 1)
                if 2 <= s <= NH + 1:
                    g = s - 2
                    act.wait_ge(*done(f"transposes {g}"))
                    if g >= 2:
                        act.wait_ge(*done(f"values {g - 2}"))
                    nc.scalar.activation(PT[:, g % 2, 0:T1], bank[4][0:96, 0:T1], ACT.Copy)\
                        .then_inc(*S.step(f"transposed a {g}"))
                if s < NH:
                    act.wait_ge(*done(f"neg max {s}"))
                    X, Y = bank[s % 2], bank[2 + s % 2]
                    for t, src in enumerate((X[0:96, 0:96], X[0:96, 96:288], Y[0:80, 0:T1])):
                        nq, at, w = QT[t][1], (0, 96, 288)[t], src.shape[1]
                        step = S.step(f"exp {s}")
                        nc.scalar.activation(Pp[0:nq, s % 2, at:at + w], src, ACT.Exp, bias=nb[0:nq, s % 2, t:t + 1],
                                             scale=SCALE, accum_out=sm[0:nq, s % 2, t:t + 1]).then_inc(*step)
                if s >= 4 and s % 2 == 0:
                    pair = (s - 4) // 2
                    act.wait_ge(*done(f"values {2 * pair + 1}"))
                    nc.scalar.activation(uh[:, pair, :], bank[6 + pair % 2][:, 0:T1], ACT.Copy)\
                        .then_inc(*S.step(f"att out {pair} high"))
            for u in range(4):
                n = FIRST_UNIT["wo"] + u
                for b in range(2):
                    post("post0", 2 * u + b, n, FIRST_BLOCK["wo"] + 2 * u + b, "mix_post0")
                high(n + 2)
            for c in range(DC):
                act.wait_ge(*done(f"f0 h {c}"))
                u_high("f0", c, T1, 0, "ffn_pre0")
            ffn_up(0, T1, True)
            ffn_down(0)
            for c in range(DC):
                act.wait_ge(*done(f"a1 h {c}"))
                u_high("a1", c, T1, 0, "mix_pre1")
            act.wait_ge(*done("a1 1/rms"))
            for half in range(2):
                for t, (t0, nt_) in enumerate(TT):
                    b = FIRST_BLOCK["pool"] + half * len(TT) + t
                    block_done(b)
                    nc.scalar.activation(pz[0:nt_, t, half * 512:(half + 1) * 512], bank[BLOCKS[b]["bank"]][0:nt_, :],
                                         ACT.Copy, scale=nr[0:nt_, t:t + 1]).then_inc(freed["a"], 1)
            act.wait_ge(*done("pool gains"))
            n = FIRST_UNIT["pool"]
            for b in range(8):
                post("post1", b, n, FIRST_BLOCK["pool"] + 2 * len(TT) + b, psg[:, b:b + 1], scale=pcol("pool_scale", b))
            high(n + 2)
            for c in range(DC):
                act.wait_ge(*done(f"f1 h {c}"))
                u_high("f1", c, T1, 0, "ffn_pre1")
            ffn_up(1, T1, True)
            ffn_down(1)
            T = SEQ
            for c in range(DC):
                act.wait_ge(*done(f"g h {c}"))
                u_high("g", c, T, META, "ln1")
            n = FIRST_UNIT["gin_a"]
            high(n + 2)
            high(n + 3)
            act.wait_ge(*done("gate -|x|"))
            nc.scalar.activation(ek[:, :], eq[:, :], ACT.Exp).then_inc(*S.step())
            act.wait_ge(*S.now())
            nc.scalar.activation(ek[:, :], ek[:, :], ACT.Ln, bias=1.0).then_inc(*S.step("gate log"))
            for v in range(2):
                for t in range(2):
                    b = FIRST_BLOCK["gin_v"] + 2 * v + t
                    block_done(b)
                    act.wait_ge(*done("g 1/rms"))
                    nc.scalar.activation(gv[:, t, v * 256:(v + 1) * 256], bank[BLOCKS[b]["bank"]][:, 0:256],
                                         ACT.Copy, scale=nr[:, t:t + 1]).then_inc(freed["a"], 1)
                high(n + 4 + v)

            def level_exps(l):
                B = 1 << l
                v = lambda t, side: t[:, :].rearrange("p (n s b) -> p n s b", s=2, b=B)[:, :, side, :]
                act.wait_ge(*done(f"level {l} sums"))
                nc.scalar.activation(v(eq, 1), v(pre, 1), ACT.Exp).then_inc(*S.step(f"level {l} exp q"))
                nc.scalar.activation(v(ek, 0), v(suf, 0), ACT.Exp).then_inc(*S.step(f"level {l} exp k"))

            def conv_tap(j):
                act.wait_ge(*done(f"conv in {j}"))
                nc.scalar.activation(cv[:, 0, 0:T], ur[:, 0, 2:2 + T], ACT.Copy, scale=pcol("conv2", 8 + j))\
                    .then_inc(*S.step(f"conv tap 2 {j}"))

            def conv_y_high(j):
                act.wait_ge(*done(f"conv y {j}"))
                nc.scalar.activation(xh[:, 4 + j, 0:T], xf[:, 0:T], ACT.Copy).then_inc(*S.step(f"conv y high {j}"))

            level_exps(0)
            level_exps(1)
            high(n + 6)
            level_exps(2)
            level_exps(3)
            high(n + 7)
            level_exps(4)
            level_exps(5)
            high(n + 8)
            conv_tap(0)
            conv_y_high(0)
            level_exps(6)
            level_exps(7)
            high(n + 9)
            conv_tap(1)
            conv_y_high(1)
            act.wait_ge(*done("gla out"))
            for pair in range(2):
                src = bank[6 + pair][:, :]
                nc.scalar.activation(m[:, 4 + 2 * pair:6 + 2 * pair, 0:T], src.rearrange("p (a t) -> p a t", a=2),
                                     ACT.Copy).then_inc(*S.step())
                step = S.step("gla out squares")
                nc.scalar.activation((eq, ek)[pair][:, :], src, ACT.Square).then_inc(*step)
            high(n + 10)
            conv_tap(2)
            conv_y_high(2)
            nc.scalar.activation(m[:, 0:4, 0:T], m[:, 0:4, 0:T], ACT.Silu).then_inc(*S.step("gla gate"))
            conv_tap(3)
            high(n + 11)
            for head in range(GH):
                act.wait_ge(*done(f"gla mix {head}"))
                nc.scalar.activation(xh[:, head, 0:T], m[:, 4 + head, 0:T], ACT.Copy)\
                    .then_inc(*S.step(f"gla mix high {head}"))
            conv_y_high(3)
            for u in range(4):
                n = FIRST_UNIT["wout"] + u
                high(n + 2)
                for c in range(2 * u, 2 * u + 2):
                    act.wait_ge(freed["v"], BLOCKS[FIRST_BLOCK["wout"] + c]["freed"])
                    u_high("f2", c, T, META, "ln2")
                if u == 1:
                    act.wait_ge(p_in, 16)
                    for k in range(2):
                        nc.scalar.activation(xh[:, 8 + k, 0:T], cv[:, k, 0:T], ACT.Copy).then_inc(*S.step(f"p high {k}"))
            for b in range(8):
                block_done(FIRST_BLOCK["pproj"] + b)
                nc.scalar.activation(m[:, b, 0:T], bank[BLOCKS[FIRST_BLOCK["pproj"] + b]["bank"]][:, 0:T], ACT.Copy)\
                    .then_inc(freed["a"], 1)
            high(FIRST_UNIT["pproj"] + 2)
            ffn_up(2, T, False)
            n0, b0 = FIRST_UNIT["down2"], FIRST_BLOCK["down2"]
            with act.Fori(0, (DC - 2) // 2) as i:
                S.enter("down2", i)
                for k in range(2):
                    high(n0 + k + 2, i)
                    act.wait_ge(freed["v"], 2 * i + BLOCKS[b0 + k]["freed"])
                    u_high("e", 2 * i + k, T, META, "ln3", k, i)
                S.leave((DC - 2) // 2)
            for c in range(DC - 2, DC):
                high(n0 + c + 2)
                act.wait_ge(freed["v"], BLOCKS[b0 + c]["freed"])
                u_high("e", c, T, META, "ln3")
            for u in range(4):
                n = FIRST_UNIT["pgate"] + u
                for b in range(2):
                    c = 2 * u + b
                    act.wait_ge(freed["v"], BLOCKS[FIRST_BLOCK["pgate"] + c]["freed"])
                    nc.scalar.activation(cv[:, b, 0:T], cv[:, b, 0:T], ACT.Sigmoid).then_inc(*S.step(f"ple gate {c}"))
                if n + 2 < len(UNITS):
                    high(n + 2)
                for c in range(2 * u, 2 * u + 2):
                    act.wait_ge(*done(f"out h {c}"))
                    square("out", c, h[:, c, META:T1], T, S.step(f"out sq {c}"))

        @block.vector
        def _(dve):
            S = Steps("vector", step_sems["vector"], marks)

            def low(n, i=None, first=None, middle=None):
                cols, split = vector_cols(n), 0
                if first:
                    split = first_half(n)
                    dve.wait_ge(*done(first, i))
                    nc.vector.tensor_tensor(wl[n % 2][:, 0:split], raw[n % 2][:, 0:split],
                                            wh[n % 2][:, 0:split].bitcast(F32), ALU.subtract).then_inc(*S.step())
                if middle:
                    middle()
                dve.wait_ge(high_parts, n + 1 if i is None else 2 * i + (n + 1))
                nc.vector.tensor_tensor(wl[n % 2][:, split:cols], raw[n % 2][:, split:cols],
                                        wh[n % 2][:, split:cols].bitcast(F32), ALU.subtract).then_inc(low_parts_v, 1)

            def block_done(b, i=None, stride=0):
                dve.wait_ge(products, b + 1 if i is None else i * stride + (b + 1))

            def u_low(name, c, T, t0, gain, k=None, i=None):
                label = c if k is None else k
                dve.wait_ge(*done(f"{name} u high {label}", i))
                nc.vector.scalar_tensor_tensor(ul[:, c, 0:T], h[:, c, t0:t0 + T], pcol(gain, c),
                                               uh[:, c, 0:T].bitcast(F32), ALU.mult, ALU.subtract)\
                    .then_inc(*S.step(f"{name} u low {label}"))

            def norm(name, slices):
                n = slices[-1][1]
                dve.wait_ge(*done(f"{name} sums"))
                for c0, c1, inv in slices:
                    nc.vector.tensor_scalar(nx[:, c0:c1], bank[NORM_BANK][:, c0:c1], inv, EPS, ALU.mult, ALU.add)\
                        .then_inc(*S.step())
                dve.wait_ge(*S.now())
                x, ax, t, y = nx[:, 0:n], nh[:, 0:n], nt[:, 0:n], ny[:, 0:n]
                nc.vector.tensor_scalar(t.bitcast(I32), x.bitcast(I32), 1, None, ALU.arith_shift_right)\
                    .then_inc(*S.step())
                nc.vector.tensor_scalar(ax, x, GUESS_A * GUESS_A, None, ALU.mult).then_inc(*S.step())
                dve.wait_ge(*S.now())
                nc.vector.tensor_scalar(y.bitcast(I32), t.bitcast(I32), -1.0, float(GUESS), ALU.mult, ALU.add)\
                    .then_inc(*S.step())

                def times_y(by):
                    dve.wait_ge(*S.now())
                    nc.vector.tensor_tensor(t, y, y, ALU.mult).then_inc(*S.step())
                    dve.wait_ge(*S.now())
                    nc.vector.tensor_tensor(t, t, by, ALU.mult).then_inc(*S.step())
                    dve.wait_ge(*S.now())
                times_y(x)
                nc.vector.scalar_tensor_tensor(y, t, -GUESS_B, y, ALU.add, ALU.mult).then_inc(*S.step())
                times_y(ax)
                nc.vector.scalar_tensor_tensor(t, t, -10.0 / 3.0, t, ALU.add, ALU.mult).then_inc(*S.step())
                dve.wait_ge(*S.now())
                nc.vector.scalar_tensor_tensor(y, t, 5.0, y, ALU.add, ALU.mult).then_inc(*S.step())
                dve.wait_ge(*S.now())
                if name in ("a1", "g"):
                    nc.vector.tensor_scalar(nr[:, 0:n], y, -GUESS_A * 3.0 / 8.0, None, ALU.mult)\
                        .then_inc(*S.step(f"{name} 1/rms"))
                if name == "a1":
                    return
                for c in range(n):
                    step = S.step(f"{name} diagonal")
                    nc.vector.tensor_scalar(diag[:, c * P:(c + 1) * P], ident[:, :], ny[:, c:c + 1],
                                            -GUESS_A * 3.0 / 8.0, ALU.mult, ALU.mult).then_inc(*step)

            def one(T, a=0):
                return [(a, a + -(-T // P), 1.0 / D)]

            def keep_rows(name, T):
                dve.wait_ge(*done(f"{name} rows"))
                nc.vector.tensor_copy(rows[:, 0:T], bank[R_BANK][:, 0:T]).then_inc(*S.step())
                dve.wait_ge(*S.now())

            def scaled(out, b, sem_and_1, T, i=None, stride=0):
                block_done(b, i, stride)
                nc.vector.tensor_tensor(out, bank[BLOCKS[b]["bank"]][:, 0:T], rows[:, 0:T], ALU.mult)\
                    .then_inc(*sem_and_1)

            def freed_wait(b, i=None):
                dve.wait_ge(freed["v"], BLOCKS[b]["freed"] if i is None else 4 * i + BLOCKS[b]["freed"])

            def add_post(name, nxt, gain, T, t0, unit):
                norm(name, one(T1))
                low(unit)
                dve.wait_ge(*done(f"{name} rows"))
                for c in range(DC + 1):
                    if c < DC:
                        nc.vector.tensor_tensor(m[:, c, :], m[:, c, :], bank[R_BANK][:, 0:T1], ALU.mult)\
                            .then_inc(*S.step())
                        dve.wait_ge(*S.now())
                        nc.vector.tensor_tensor(h[:, c, :], h[:, c, :], m[:, c, :], ALU.add)\
                            .then_inc(*S.step(f"{nxt} h {c}"))
                    if c >= 1:
                        u_low(nxt, c - 1, T, t0, gain)

            def ffn_up(l, T, conv, name):
                n0 = FIRST_UNIT[f"up{l}"]
                norm(name, one(T))
                keep_rows(name, T)

                def x_full(place, of):
                    k, i = place
                    dve.wait_ge(*done(f"silu {l} {of[0]}", of[1]))
                    dve.wait_ge(*S.now())
                    value = cv[:, 1, 0:T] if conv else ur[:, 1, 2:2 + T]
                    nc.vector.tensor_tensor(xf[:, 0:T], cv[:, 0, 0:T], value, ALU.mult)\
                        .then_inc(*S.step(f"x full {l} {k}"))

                def x_low(place, j):
                    k, i = place
                    dve.wait_ge(*done(f"x high {l} {k}", i))
                    nc.vector.tensor_tensor(xl[:, j, 0:T], xf[:, 0:T], xh[:, j, 0:T].bitcast(F32), ALU.subtract)\
                        .then_inc(*S.step(f"x low {l} {k}"))

                def turn(j, place, before):
                    k, i = place
                    n = n0 + (j if i is None else 2 + int(k[1]))
                    b = UNITS[n]["first"]
                    dve.wait_ge(*S.now())
                    scaled(ur[:, 0, 2:2 + T], b, (freed["v"], 1), T, i, 4)
                    scaled(ur[:, 1, 2:2 + T], b + 1, (freed["v"], 1), T, i, 4)
                    if conv:
                        if before is not None:
                            x_full(place, before)
                        low(n + 2, i, f"first high {l} {k}")
                        for tap in (1, 0):
                            for hf in range(2):
                                if tap == 1:
                                    dve.wait_ge(*done(f"tap 2 {l} {hf} {k}", i))
                                elif hf == 0:
                                    dve.wait_ge(*S.now())
                                nc.vector.scalar_tensor_tensor(
                                    cv[:, hf, 0:T], ur[:, hf, tap:tap + T], pcol(f"cw{l}", (tap * 2 + hf) * FC + j),
                                    cv[:, hf, 0:T], ALU.mult, ALU.add).then_inc(*S.step(f"taps {l} {hf} {k}"))
                        if before is not None:
                            x_low(place, j - 1)
                    else:
                        def full():
                            freed_wait(b + 1, i)
                            x_full(place, place)
                        low(n + 2, i, f"first high {l} {k}", full)
                        x_low(place, j)

                up_turns(dve, S, l, turn)
                if conv:
                    x_full(up_place(FC), up_place(FC - 1))
                    x_low(up_place(FC), FC - 1)

            def ffn_down_lows(l):
                n0 = FIRST_UNIT[f"down{l}"]
                with dve.Fori(0, (DC - 2) // 2) as i:
                    for k in range(2):
                        low(n0 + k + 2, i)
                low(n0 + DC)

            nc.vector.memset(ones[:, :], 1.0).then_inc(*S.step())
            nc.vector.memset(ur[:, :, :], 0.0).then_inc(*S.step())
            nc.vector.memset(mx[:, :, :], 0.0).then_inc(*S.step())
            nc.vector.memset(sm[:, :, :], 1.0).then_inc(*S.step())
            nc.vector.memset(sq[:, :, :], 0.0).then_inc(*S.step())
            nc.vector.memset(acc[:, :, :], 0.0).then_inc(*S.step("constants"))
            for p, cols in enumerate(first_pieces()):
                if p < PIECES - 1:
                    dve.wait_ge(*done(f"first high {p}"))
                    signal = (low_parts_v, 1) if p == PIECES - 2 else S.step(f"first low {p}")
                    nc.vector.tensor_tensor(wl[0][:, cols], raw[0][:, cols], wh[0][:, cols].bitcast(F32),
                                            ALU.subtract).then_inc(*signal)
                for c in range(2 * p, 2 * p + 2):
                    u_low("a0", c, T1, 0, "mix_pre0")
            low(1)
            dve.wait_ge(tables_in, 64)
            norm("a0", one(T1))
            low(2)
            keep_rows("a0", T1)
            nc.vector.tensor_tensor(psg[:, :], pcol("pool_scale", 0, 8), pcol("mix_post1", 0, 8), ALU.mult)\
                .then_inc(*S.step("pool gains"))
            for hf in range(2):
                nc.vector.tensor_tensor(ropeR[:, hf, :], rope[:, hf, :], rows[:, :], ALU.mult).then_inc(*S.step())
            for j in range(QC + KC):
                scaled(m[:, j, :], FIRST_BLOCK["dq"] + j, (freed["v"], 1), T1)
            norm("c", [(0, 3, 1.0 / QR), (3, 6, 1.0 / KVR)])
            low(3)
            dve.wait_ge(*done("c rows"))
            for j in range(QC + KC + 1):
                if j < QC + KC:
                    r = bank[R_BANK][:, 0:T1] if j < QC else bank[NORM_BANK][:, P:P + T1]
                    nc.vector.tensor_tensor(m[:, j, :], m[:, j, :], r, ALU.mult).then_inc(*S.step(f"latent {j}"))
                if j >= 1:
                    c = j - 1
                    dve.wait_ge(*done(f"c u high {c}"))
                    g = pcol("q_norm", c) if c < QC else pcol("kv_norm", c - QC)
                    nc.vector.scalar_tensor_tensor(ul[:, c, :], m[:, c, :], g, uh[:, c, :].bitcast(F32),
                                                   ALU.mult, ALU.subtract).then_inc(*S.step(f"c u low {c}"))
            b = FIRST_BLOCK["dkr"]
            dve.wait_ge(*S.now())
            for hf, dst in ((0, kr), (1, rb)):
                block_done(b + hf)
                nc.vector.tensor_tensor(dst[:, :], bank[BLOCKS[b + hf]["bank"]][:, 0:T1], ropeR[:, hf, :], ALU.mult)\
                    .then_inc(freed["v"], 1)
            freed_wait(b + 1)
            nc.vector.tensor_tensor(kr[:, :], kr[:, :], rb[:, :], ALU.add).then_inc(*S.step("k rope full"))
            low(4)
            low(5)
            for q4 in range(4):
                b = FIRST_BLOCK["uqr"] + 2 * q4
                for hf, dst in ((0, ra), (1, rb)):
                    block_done(b + hf)
                    if hf == 0:
                        dve.wait_ge(*S.now())
                    nc.vector.tensor_tensor(dst[:, :], bank[BLOCKS[b + hf]["bank"]][:, 0:T1], rope[:, hf, :], ALU.mult)\
                        .then_inc(freed["v"], 1)
                freed_wait(b + 1)
                for j in range(4):
                    part = slice(32 * j, 32 * j + 32)
                    nc.vector.tensor_tensor(Q[64:96, 4 * q4 + j, :], ra[part, :], rb[part, :], ALU.add)\
                        .then_inc(*S.step())
            low(6)
            for half in range(2):
                for t, (q0, nq) in enumerate(QT):
                    if half == 1 and t == 0:
                        low(7)
                    b = FIRST_BLOCK["uv"] + half * 3 + t
                    block_done(b)
                    nc.vector.tensor_copy(V[0:nq, t, half * 512:(half + 1) * 512], bank[BLOCKS[b]["bank"]][0:nq, :])\
                        .then_inc(freed["v"], 1)
            for s in range(NH + 4):
                if s == 3:
                    low(FIRST_UNIT["wo"] + 1)
                if s < NH:
                    X, Y, p = bank[s % 2], bank[2 + s % 2], s % 2
                    dve.wait_ge(*done(f"scores {s}"))
                    dv = X[0:96, 0:384].rearrange("q (a b) -> q a b", a=2)[:, :, 0:96]
                    nc.vector.tensor_tensor(dv, dv, cmask[:, :].unsqueeze(1).to_broadcast([96, 2, 96]), ALU.add)\
                        .then_inc(*S.step())
                    nc.vector.tensor_tensor(Y[0:80, 192:T1], Y[0:80, 192:T1], cmask[0:80, 0:80], ALU.add)\
                        .then_inc(*S.step())
                    dve.wait_ge(*S.now())
                    for t, src in enumerate((X[0:96, 0:96], X[0:96, 96:288], Y[0:80, 0:T1])):
                        nc.vector.reduce_max(mx[0:QT[t][1], p, t:t + 1], src, AX).then_inc(*S.step())
                    dve.wait_ge(*S.now())
                    nc.vector.tensor_scalar(nb[:, p, :], mx[:, p, :], -SCALE, None, ALU.mult)\
                        .then_inc(*S.step(f"neg max {s}"))
                if 2 <= s <= NH + 1:
                    g = s - 2
                    dve.wait_ge(*done(f"transposes {g}"))
                    if g >= 2:
                        dve.wait_ge(*done(f"values {g - 2}"))
                    nc.vector.tensor_copy(PT[0:96, g % 2, T1:T1 + 176], bank[5][0:96, 0:176]).then_inc(*S.step())
                    nc.vector.tensor_copy(PT[0:80, g % 2, 448:528], bank[5][0:80, 176:256])\
                        .then_inc(*S.step(f"transposed b {g}"))
                if 1 <= s <= NH:
                    g, p = s - 1, (s - 1) % 2
                    dve.wait_ge(*done(f"exp {g}"))
                    nc.vector.reciprocal(rc[:, p, :], sm[:, p, :]).then_inc(*S.step())
                    dve.wait_ge(*S.now())
                    for t, w in enumerate((96, 192, T1)):
                        nq, at = QT[t][1], (0, 96, 288)[t]
                        step = S.step(f"probs {g}")
                        nc.vector.tensor_scalar(Pp[0:nq, p, at:at + w], Pp[0:nq, p, at:at + w], rc[0:nq, p, t:t + 1],
                                                None, ALU.mult).then_inc(*step)
                if s >= 4 and s % 2 == 0:
                    pair = (s - 4) // 2
                    dve.wait_ge(*done(f"att out {pair} high"))
                    nc.vector.tensor_tensor(ul[:, pair, :], bank[6 + pair % 2][:, 0:T1], uh[:, pair, :].bitcast(F32),
                                            ALU.subtract).then_inc(*S.step(f"att out {pair} low"))
            for u in range(3):
                low(FIRST_UNIT["wo"] + u + 2)
            add_post("post0", "f0", "ffn_pre0", T1, 0, FIRST_UNIT["wo"] + 5)
            ffn_up(0, T1, True, "f0")
            ffn_down_lows(0)
            add_post("fpost0", "a1", "mix_pre1", T1, 0, FIRST_UNIT["down0"] + DC + 1)

            norm("a1", one(T1))
            add_post("post1", "f1", "ffn_pre1", T1, 0, FIRST_UNIT["pool"] + 2)
            ffn_up(1, T1, True, "f1")
            ffn_down_lows(1)
            T = SEQ
            add_post("fpost1", "g", "ln1", T, META, FIRST_UNIT["down1"] + DC + 1)

            norm("g", one(T))
            keep_rows("g", T)
            n, b = FIRST_UNIT["gin_a"], FIRST_BLOCK["gin_a"]
            scaled(glr[:, :], b, (freed["v"], 1), T)
            for pair in range(2):
                block_done(b + 1 + pair)
                nc.vector.scalar_tensor_tensor(gq[:, pair * T:(pair + 1) * T], bank[BLOCKS[b + 1 + pair]["bank"]][:, 0:T],
                                               float(GDK) ** -0.5, rows[:, 0:T], ALU.mult, ALU.mult)\
                    .then_inc(freed["v"], 1)
            low(n + 2)
            for pair in range(2):
                scaled(gk[:, pair * T:(pair + 1) * T], FIRST_BLOCK["gin_k"] + pair, (freed["v"], 1), T)
            low(n + 3)
            dve.wait_ge(*done("gate logits"))
            for pair in range(2):
                nc.vector.tensor_scalar(pre[:, pair * T:(pair + 1) * T], bank[6][:, pair * T:(pair + 1) * T],
                                        pcol("b_gate", pair), None, ALU.add).then_inc(*S.step())
            dve.wait_ge(*S.now())
            nc.vector.scalar_tensor_tensor(eq[:, :], pre[:, :], -1.0, pre[:, :], ALU.mult, ALU.min)\
                .then_inc(*S.step("gate -|x|"))
            for t in (suf, ql, kl):
                nc.vector.memset(t[:, :], 0.0).then_inc(*S.step())
            nc.vector.memset(Sd[:, :, :], 0.0).then_inc(*S.step("gate inputs"))
            dve.wait_ge(*done("gate log"))
            nc.vector.scalar_tensor_tensor(pre[:, :], pre[:, :], 0.0, ek[:, :], ALU.min, ALU.subtract)\
                .then_inc(*S.step())
            dve.wait_ge(*S.now())
            nc.vector.tensor_scalar(pre[:, :], pre[:, :], 1.0 / 16.0, None, ALU.mult).then_inc(*S.step("level 0 sums"))
            for v in range(2):
                low(n + 4 + v)

            def level_operands(l):
                B = 1 << l
                v = lambda t, side: t[:, :].rearrange("p (n s b) -> p n s b", s=2, b=B)[:, :, side, :]
                if l > 0:
                    dve.wait_ge(*done(f"level {LEVEL_BEFORE[l]} scores"))
                dve.wait_ge(*done(f"level {l} exp q"))
                nc.vector.tensor_tensor(v(ql, 1), v(gq, 1), v(eq, 1), ALU.mult).then_inc(*S.step(f"level {l} q"))
                dve.wait_ge(*done(f"level {l} exp k"))
                nc.vector.tensor_tensor(v(kl, 0), v(gk, 0), v(ek, 0), ALU.mult).then_inc(*S.step(f"level {l} k"))
                if l < FAR:
                    nb_ = 2 * SEQ // (2 * B)
                    total = lambda side: v(pre, side)[:, :, B - 1:B].to_broadcast([P, nb_, B])
                    nc.vector.tensor_tensor(v(suf, 0), v(suf, 0), total(1), ALU.add).then_inc(*S.step())
                    dve.wait_ge(*S.now())
                    nc.vector.tensor_tensor(v(pre, 1), v(pre, 1), total(0), ALU.add)\
                        .then_inc(*S.step(f"level {l + 1} sums"))

            def level_kept(l):
                dve.wait_ge(*done(f"level {l} scores"))
                if l == DIAGONAL:
                    dve.wait_ge(*S.now())
                    dve.wait_ge(tables_in, 16 * 7)
                for half in range(2):
                    if l == FAR:
                        nc.vector.tensor_copy(S01[:, half, :], bank[6 + half][:, 0:2 * P]).then_inc(*S.step(f"level {l} kept {half}"))
                    else:
                        mask = lmask[:, min(l, 7), :].unsqueeze(1).to_broadcast([P, 4, P])
                        nc.vector.copy_predicated(Sd[:, half, :].rearrange("p (a t) -> p a t", a=4), mask,
                                                  bank[6 + half][:, :].rearrange("p (a t) -> p a t", a=4))\
                            .then_inc(*S.step(f"level {l} kept {half}"))
                dve.wait_ge(*S.now())

            def conv_in(j):
                b = FIRST_BLOCK["gin_c"] + 3 * j
                scaled(ur[:, 0, 2:2 + T], b, (freed["v"], 1), T)
                scaled(ur[:, 1, 2:2 + T], b + 1, (freed["v"], 1), T)
                scaled(xf[:, 0:T], b + 2, (freed["v"], 1), T)
                freed_wait(b + 1)
                nc.vector.tensor_tensor(ur[:, 0, 2:2 + T], ur[:, 0, 2:2 + T], ur[:, 1, 2:2 + T], ALU.mult)\
                    .then_inc(*S.step(f"conv in {j}"))

            def conv_y(j):
                dve.wait_ge(*done(f"conv tap 2 {j}"))
                for tap in (1, 0):
                    nc.vector.scalar_tensor_tensor(cv[:, 0, 0:T], ur[:, 0, tap:tap + T], pcol("conv2", 4 * tap + j),
                                                   cv[:, 0, 0:T], ALU.mult, ALU.add).then_inc(*S.step())
                    dve.wait_ge(*S.now())
                freed_wait(FIRST_BLOCK["gin_c"] + 3 * j + 2)
                nc.vector.tensor_tensor(xf[:, 0:T], xf[:, 0:T], cv[:, 0, 0:T], ALU.mult).then_inc(*S.step(f"conv y {j}"))

            def conv_y_low(j):
                dve.wait_ge(*done(f"conv y high {j}"))
                nc.vector.tensor_tensor(xl[:, 4 + j, 0:T], xf[:, 0:T], xh[:, 4 + j, 0:T].bitcast(F32), ALU.subtract)\
                    .then_inc(*S.step(f"conv y low {j}"))
                dve.wait_ge(*S.now())

            def gates(v):
                for c in range(2):
                    scaled(m[:, 2 * v + c, 0:T], FIRST_BLOCK["gin_g"] + 2 * v + c, (freed["v"], 1), T)

            level_kept(DIAGONAL)
            level_operands(0)
            gates(0)
            level_kept(0)
            level_operands(1)
            low(n + 6)
            level_kept(1)
            level_operands(2)
            gates(1)
            level_kept(2)
            level_operands(3)
            low(n + 7)
            level_kept(3)
            level_operands(4)
            for j in range(4):
                conv_in(j)
                if j < 2:
                    level_kept(4 + 2 * j)
                    level_operands(5 + 2 * j)
                if j == 3:
                    dve.wait_ge(*done("gn rows"))
                    for pair in range(2):
                        o = m[:, 4 + 2 * pair:6 + 2 * pair, 0:T]
                        nc.vector.tensor_tensor(o, o, bank[6 + pair][:, :].rearrange("p (a t) -> p a t", a=2), ALU.mult)\
                            .then_inc(*S.step())
                    dve.wait_ge(*done("gla gate"))
                    dve.wait_ge(*S.now())
                    for head in range(GH):
                        o = m[:, 4 + head, 0:T]
                        nc.vector.scalar_tensor_tensor(o, o, pcol("gn"), m[:, head, 0:T], ALU.mult, ALU.mult)\
                            .then_inc(*S.step(f"gla mix {head}"))
                    for head in range(GH):
                        dve.wait_ge(*done(f"gla mix high {head}"))
                        nc.vector.tensor_tensor(xl[:, head, 0:T], m[:, 4 + head, 0:T], xh[:, head, 0:T].bitcast(F32),
                                                ALU.subtract).then_inc(*S.step(f"gla mix low {head}"))
                else:
                    low(n + 8 + j)
                conv_y(j)
                conv_y_low(j)
                if j < 2:
                    level_kept(5 + 2 * j)
                if j == 0:
                    level_operands(6)
                if j == 2:
                    norm("gn", [(0, 8, 1.0 / GDV)])
                if j == 3:
                    low(n + 8 + j)

            def add_block(c, b, i=None, stride=0):
                block_done(b, i, stride)
                nc.vector.tensor_tensor(h[:, c, META:T1], h[:, c, META:T1], bank[BLOCKS[b]["bank"]][:, 0:T], ALU.add)\
                    .then_inc(freed["v"], 1)

            for u in range(4):
                for c in range(2 * u, 2 * u + 2):
                    add_block(c, FIRST_BLOCK["wout"] + c)
                low(FIRST_UNIT["wout"] + u + 2)
                for c in range(2 * u, 2 * u + 2):
                    u_low("f2", c, T, META, "ln2")
                if u == 1:
                    for k in range(2):
                        dve.wait_ge(*done(f"p high {k}"))
                        nc.vector.tensor_tensor(xl[:, 8 + k, 0:T], cv[:, k, 0:T], xh[:, 8 + k, 0:T].bitcast(F32),
                                                ALU.subtract).then_inc(*S.step(f"p low {k}"))
            low(FIRST_UNIT["pproj"] + 2)
            ffn_up(2, T, False, "f2")
            n0, b0 = FIRST_UNIT["down2"], FIRST_BLOCK["down2"]
            with dve.Fori(0, (DC - 2) // 2) as i:
                S.enter("down2", i)
                for k in range(2):
                    add_block(2 * i + k, b0 + k, i, 2)
                    low(n0 + k + 2, i)
                    u_low("e", 2 * i + k, T, META, "ln3", k, i)
                S.leave((DC - 2) // 2)
            for c in range(DC - 2, DC):
                add_block(c, b0 + c)
                low(n0 + c + 2)
                u_low("e", c, T, META, "ln3")
            norm("e", one(T))
            keep_rows("e", T)
            for u in range(4):
                n = FIRST_UNIT["pgate"] + u
                for b in range(2):
                    scaled(cv[:, b, 0:T], FIRST_BLOCK["pgate"] + 2 * u + b, (freed["v"], 1), T)
                if n + 2 < len(UNITS):
                    low(n + 2)
                for b in range(2):
                    c = 2 * u + b
                    dve.wait_ge(*done(f"ple gate {c}"))
                    nc.vector.tensor_tensor(cv[:, b, 0:T], cv[:, b, 0:T], m[:, c, 0:T], ALU.mult).then_inc(*S.step())
                    dve.wait_ge(*S.now())
                    nc.vector.tensor_tensor(h[:, c, META:T1], h[:, c, META:T1], cv[:, b, 0:T], ALU.add)\
                        .then_inc(*S.step(f"out h {c}"))
                dve.wait_ge(*S.now())
            norm("out", one(T))
            dve.wait_ge(*done("out rows"))
            for c in range(DC):
                nc.vector.scalar_tensor_tensor(m[:, c, 0:T], h[:, c, META:T1], pcol("lnf", c), bank[R_BANK][:, 0:T],
                                               ALU.mult, ALU.mult).then_inc(*S.step(f"final {c}"))

        @block.gpsimd
        def _(pool):
            S = Steps("pool", step_sems["pool"], marks)

            def low(n, i=None):
                at = slice(vector_cols(n), UNITS[n]["tiles"] * P)
                pool.wait_ge(high_parts, n + 1 if i is None else 2 * i + (n + 1))
                nc.gpsimd.tensor_tensor(wl[n % 2][:, at], raw[n % 2][:, at], wh[n % 2][:, at].bitcast(F32),
                                        ALU.subtract).then_inc(low_parts_g, 1)

            def clear(after, T=T1):
                pool.wait_ge(*done(f"{after} sums"))
                nc.gpsimd.memset(acc[:, 0, 0:T], 0.0).then_inc(*S.step())

            def add_square(name, c, T, ready, a=0, k=None):
                label = c if k is None else k
                pool.wait_ge(*ready)
                pool.wait_ge(*S.now())
                step = S.step(f"{name} acc {label}")
                nc.gpsimd.tensor_tensor(acc[:, a, 0:T], acc[:, a, 0:T], sq[:, label % 2, 0:T], ALU.add).then_inc(*step)

            def up_lows(l):
                n0 = FIRST_UNIT[f"up{l}"]
                with pool.Fori(0, (FC - 2) // 2) as i:
                    for k in range(2):
                        low(n0 + k + 2, i)
                for j in range(FC - 2, FC):
                    low(n0 + j + 2)

            def down(l):
                n0, b0, name = FIRST_UNIT[f"down{l}"], FIRST_BLOCK[f"down{l}"], f"fpost{l}"
                with pool.Fori(0, (DC - 2) // 2) as i:
                    S.enter(f"down{l}", i)
                    for k in range(2):
                        add_square(name, 2 * i + k, T1, done(f"{name} sq {k}", i), k=k)
                        low(n0 + k + 2, i)
                    S.leave((DC - 2) // 2)
                for c in range(DC - 2, DC):
                    if c < DC - 1:
                        add_square(name, c, T1, done(f"{name} sq {c}"))
                    low(n0 + c + 2)

            pool.wait_ge(*done("constants"))
            for c in range(DC - 1):
                add_square("a0", c, T1, done(f"a0 sq {c}"))
            low(0)
            low(1)
            clear("a0")
            low(2)
            for j in range(QC + KC):
                pool.wait_ge(*done(f"latent sq {j}"))
                pool.wait_ge(*S.now())
                step = S.step("kv squares" if j == QC + KC - 1 else f"latent acc {j}")
                a = 0 if j < QC else 1
                nc.gpsimd.tensor_tensor(acc[:, a, 0:T1], acc[:, a, 0:T1], sq[:, j % 2, 0:T1], ALU.add).then_inc(*step)
            for n in range(3, 9):
                low(n)
            clear("c")
            for u in range(4):
                for c in range(2 * u, min(2 * u + 2, DC - 1)):
                    add_square("post0", c, T1, done(f"post0 sq {c}"))
                low(FIRST_UNIT["wo"] + u + 2)
            clear("post0")
            for c in range(DC - 1):
                add_square("f0", c, T1, done(f"f0 sq {c}"))
            up_lows(0)
            clear("f0")
            down(0)
            clear("fpost0")
            for c in range(DC - 1):
                add_square("a1", c, T1, done(f"a1 sq {c}"))
            clear("a1")
            for b in range(DC - 1):
                add_square("post1", b, T1, done(f"post1 sq {b}"))
            low(FIRST_UNIT["pool"] + 2)
            clear("post1")
            for c in range(DC - 1):
                add_square("f1", c, T1, done(f"f1 sq {c}"))
            up_lows(1)
            clear("f1")
            down(1)
            T = SEQ
            clear("fpost1")
            for c in range(DC - 1):
                add_square("g", c, T, done(f"g sq {c}"))
            for n in range(FIRST_UNIT["gin_a"] + 2, FIRST_UNIT["gin_c"] + 6):
                low(n)
            clear("g")
            for u in range(4):
                low(FIRST_UNIT["wout"] + u + 2)
                for c in range(2 * u, min(2 * u + 2, DC - 1)):
                    add_square("f2", c, T, done(f"f2 sq {c}"))
            low(FIRST_UNIT["pproj"] + 2)
            up_lows(2)
            clear("f2")
            n0 = FIRST_UNIT["down2"]
            with pool.Fori(0, (DC - 2) // 2) as i:
                S.enter("down2", i)
                for k in range(2):
                    low(n0 + k + 2, i)
                    add_square("e", 2 * i + k, T, done(f"e sq {k}", i), k=k)
                S.leave((DC - 2) // 2)
            for c in range(DC - 2, DC):
                low(n0 + c + 2)
                if c < DC - 1:
                    add_square("e", c, T, done(f"e sq {c}"))
            low(FIRST_UNIT["pgate"] + 2)
            low(FIRST_UNIT["pgate"] + 3)
            clear("e")
            for c in range(DC - 1):
                add_square("out", c, T, done(f"out sq {c}"))


def _tiles(w, nb, order="kb"):
    kc, units = w.shape[0] // P, w.shape[1] // (nb * P)
    return np.ascontiguousarray(w.reshape(kc, P, units, nb * P).transpose(2, 1, 0, 3)).reshape(units, P, kc * nb * P)


def _columns(v):
    return np.ascontiguousarray(v.reshape(-1, P).T)


def _layout(x):
    f = lambda name: np.asarray(x[name])
    a = {}
    h0 = np.concatenate([f("meta_tokens"), f("x")[0]], axis=0)
    a["h0"] = np.ascontiguousarray(h0.T.reshape(DC, P, T1).transpose(1, 0, 2))
    a["p_t"] = np.ascontiguousarray(f("p_2")[0, 0].T.reshape(2, P, SEQ).transpose(1, 0, 2))
    a["wgu"] = f("w_gate_up_2")[0]
    dqkv = f("mla_w_dqkv")[0]
    a["w_dq"] = _tiles(dqkv[:, 0:QR], 3)
    a["w_dkv"] = _tiles(dqkv[:, QR:QR + KVR], 2)
    krope = np.arange(QR + KVR, QR + KVR + ROPE)
    swap = np.r_[ROPE // 2:ROPE, 0:ROPE // 2]
    a["w_dkr"] = _tiles(dqkv[:, np.r_[np.tile(krope, 4), np.tile(krope[swap], 4)]], 2)
    uq = f("mla_w_uq")[0]
    qd = NOPE + ROPE
    a["w_uqn"] = _tiles(uq[:, np.concatenate([np.arange(NOPE) + i * qd for i in range(NH)])], 8)
    cols = []
    for q4 in range(4):
        for part in (np.arange(ROPE), swap):
            cols += [NOPE + part + i * qd for i in range(4 * q4, 4 * q4 + 4)]
    a["w_uqr"] = _tiles(uq[:, np.concatenate(cols)], 8)
    ukv = f("mla_w_ukv")[0]
    a["w_uk"] = _tiles(ukv[:, np.concatenate([np.arange(NOPE) + i * (NOPE + VD) for i in range(NH)])], 8)
    a["w_uv"] = _tiles(ukv[:, np.concatenate([NOPE + np.arange(VD) + i * (NOPE + VD) for i in range(NH)])], 8)
    a["w_wo"] = _tiles(f("mla_w_o")[0], 2)
    pw = f("pool_w_group")[0]
    a["w_pool"] = np.ascontiguousarray(pw.reshape(4, 2, P, 2, P).transpose(2, 0, 1, 3, 4)).reshape(1, P, 16 * P)
    for l, up, down in ((0, f("ffn_w_up")[0], f("ffn_w_down")[0]), (1, f("ffn_w_up")[1], f("ffn_w_down")[1]),
                        (2, f("w_gate_upffn_2")[0], f("w_down_2")[0])):
        a[f"w_up{l}"] = np.ascontiguousarray(up.reshape(DC, P, 2, FC, P).transpose(3, 1, 0, 2, 4)).reshape(FC, P, 16 * P)
        a[f"w_down{l}"] = _tiles(down, 1)
    gin = f("w_in_2")[0]
    o = np.cumsum([0, 256, 256, 512, 512, 16, 512, 512, 512])
    a["w_gin_a"] = _tiles(gin[:, np.r_[np.tile(np.arange(o[4], o[5]), 8), o[0]:o[1]]], 3)
    a["w_gin_k"] = _tiles(gin[:, o[1]:o[2]], 2)
    a["w_gin_v"] = _tiles(gin[:, o[2]:o[3]], 2)
    a["w_gin_g"] = _tiles(gin[:, o[3]:o[4]], 2)
    conv = [np.r_[o[6] + j * P:o[6] + (j + 1) * P, o[7] + j * P:o[7] + (j + 1) * P, o[5] + j * P:o[5] + (j + 1) * P]
            for j in range(4)]
    a["w_gin_c"] = _tiles(gin[:, np.concatenate(conv)], 3)
    a["w_wout"] = _tiles(f("w_out_2")[0], 2)
    a["w_pproj"] = _tiles(f("w_ple_proj_2")[0], 8)
    a["w_pgate"] = _tiles(f("w_ple_gate_2")[0], 2)
    par = {}
    for l in range(2):
        par[f"mix_pre{l}"], par[f"mix_post{l}"] = f("norm_mix_pre")[l], f("norm_mix_post")[l]
        par[f"ffn_pre{l}"], par[f"ffn_post{l}"] = f("norm_ffn_pre")[l], f("norm_ffn_post")[l]
        par[f"cw{l}"], par[f"cb{l}"] = f("ffn_conv_w")[l], f("ffn_conv_b")[l]
    par.update(q_norm=f("mla_q_norm")[0], kv_norm=f("mla_kv_norm")[0], pool_scale=f("pool_scale")[0],
               ln1=f("ln1_g_2")[0], ln2=f("ln2_g_2")[0], ln3=f("ln3_g_2")[0], lnf=f("lnf_g_2"),
               b_gate=f("b_gate_2")[0], conv2=f("conv_w_2")[0], gn=f("gn_g_2")[0])
    a["par"] = np.ascontiguousarray(np.concatenate([_columns(par[name]) for name in PCOLS], axis=1))
    a["ident"] = np.eye(P, dtype=np.float32)
    inv = (1.0 / (np.float32(10000.0) ** (np.arange(0, ROPE, 2, dtype=np.float32) / ROPE))).astype(np.float32)
    ang = (np.arange(T1, dtype=np.float32)[:, None] * inv[None, :]).astype(np.float32)
    cos, sin = np.cos(ang).T, np.sin(ang).T
    a["rope"] = np.ascontiguousarray(np.stack([np.tile(cos, (8, 1)), np.tile(np.concatenate([-sin, sin]), (4, 1))], axis=1)
                                     .astype(np.float32))
    q, k = np.indices((96, 96))
    a["cmask"] = np.where(q >= k, 0.0, -1e30).astype(np.float32)
    t, t2 = np.indices((T1, T1))
    windows = []
    for w in WINDOWS:
        mean = np.where((t <= t2) & (t > t2 - w), 1.0 / np.minimum(t2 + 1, w), 0.0) - (t == t2)
        tiles = np.zeros((P, WIN))
        for i, (t0, n) in enumerate(TT):
            tiles[0:n, WIN_AT[i]:WIN_AT[i] + T1 - t0] = mean[t0:t0 + n, t0:]
        windows.append(tiles)
    a["window_means"] = np.ascontiguousarray(np.stack(windows, axis=1).astype(np.float32))
    s, t = np.indices((P, P))
    masks = [(s >> (l + 1) == t >> (l + 1)) & ((s >> l) % 2 == 0) & ((t >> l) % 2 == 1) for l in range(7)] + [s == t]
    a["lmask"] = np.ascontiguousarray(np.stack(masks, axis=1).astype(np.int32))
    return a


def kernel(**inputs):
    import concourse.bacc as bacc
    from concourse.bass_utils import run_bass_kernel_spmd

    arrays = _layout(inputs)
    marks = {}
    for final in (False, True):
        nc = bacc.Bacc("TRN2", target_bir_lowering=False, num_devices=1)
        dram = {name: nc.dram_tensor(f"{name}_dram", a.shape, mybir.dt.from_np(a.dtype), kind="ExternalInput").ap()
                for name, a in arrays.items()}
        dram["out"] = nc.dram_tensor("out_dram", (P, DC, SEQ), F32, kind="ExternalOutput").ap()
        program(nc, dram, marks, final)
    r = run_bass_kernel_spmd(nc, [{f"{name}_dram": a for name, a in arrays.items()}], core_ids=[0])
    out = np.asarray(r.results[0]["out_dram"])
    return np.ascontiguousarray(out.transpose(2, 1, 0).reshape(1, SEQ, D))
```
